# Optimizing a Trainium2 kernel written in Bass

```python
import math
import jax, jax.numpy as jnp
from jax import lax
import numpy as np

D_MODEL = 1024
BATCH = 1
SEQ = 256
DEPTH = 2

HEAD_DIM = 64
N_DIFF_HEADS = 4
DIFF_V_DIM = 2 * HEAD_DIM
DIFF_QK = N_DIFF_HEADS * 2 * HEAD_DIM
DIFF_WIDTH = N_DIFF_HEADS * DIFF_V_DIM
N_FOX_HEADS = 8
FOX_WIDTH = N_FOX_HEADS * HEAD_DIM
N_BUCKETS = 32
MAX_DISTANCE = 128
Q_BLOCK = 128
N_KEYS = 128
N_EXPERTS = N_KEYS * N_KEYS
PEER_HEADS = 8
PEER_TOPK = 16
PEER_QDIM = 256
PEER_HALF = PEER_QDIM // 2
TOKEN_BLOCK = 128
EPS = 1e-6
IN_SIZES = (DIFF_QK, DIFF_QK, DIFF_WIDTH, FOX_WIDTH, FOX_WIDTH, FOX_WIDTH, N_FOX_HEADS, D_MODEL, D_MODEL)
IN_WIDTH = sum(IN_SIZES)


def rms_norm(x, g):
    xf = x.astype(jnp.float32)
    y = xf * lax.rsqrt(jnp.mean(xf * xf, axis=-1, keepdims=True) + EPS)
    return (y * g.astype(jnp.float32)).astype(x.dtype)

def t5_bucket(dist):
    n = jnp.maximum(dist, 0)
    max_exact = N_BUCKETS // 2
    nf = jnp.maximum(n, 1).astype(jnp.float32)
    large = max_exact + (jnp.log(nf / max_exact) / math.log(MAX_DISTANCE / max_exact)
                         * (N_BUCKETS - max_exact)).astype(jnp.int32)
    large = jnp.minimum(large, N_BUCKETS - 1)
    return jnp.where(n < max_exact, n, large)

def diff_attention(q, k, v, rel_bias, lam, lam_init, subln_g):
    B, S = q.shape[0], q.shape[1]
    scale = HEAD_DIM ** -0.5
    lf = lam.astype(jnp.float32)
    lam_full = jnp.exp(jnp.sum(lf[0] * lf[1])) - jnp.exp(jnp.sum(lf[2] * lf[3])) + lam_init
    outs = []
    for blk in range(S // Q_BLOCK):
        q0 = blk * Q_BLOCK
        end = q0 + Q_BLOCK
        logits = jnp.einsum('bqhmd,bkhmd->bhmqk', q[:, q0:end], k[:, :end]).astype(jnp.float32) * scale
        dist = (q0 + jnp.arange(Q_BLOCK))[:, None] - jnp.arange(end)[None, :]
        bias = jnp.transpose(rel_bias[t5_bucket(dist)], (2, 0, 1))[:, None]
        logits = jnp.where(dist >= 0, logits + bias.astype(jnp.float32), -jnp.inf)
        probs = jax.nn.softmax(logits, axis=-1)
        weights = probs[:, :, 0] - lam_full * probs[:, :, 1]
        outs.append(jnp.einsum('bhqk,bkhd->bqhd', weights.astype(v.dtype), v[:, :end]))
    o = jnp.concatenate(outs, axis=1)
    o = rms_norm(o, subln_g) * (1.0 - lam_init)
    return o.reshape(B, S, DIFF_WIDTH)

def forgetting_attention(q, k, v, f_logit):
    B, S = q.shape[0], q.shape[1]
    scale = HEAD_DIM ** -0.5
    c = jnp.swapaxes(jnp.cumsum(jax.nn.log_sigmoid(f_logit.astype(jnp.float32)), axis=1), 1, 2)
    outs = []
    for blk in range(S // Q_BLOCK):
        q0 = blk * Q_BLOCK
        end = q0 + Q_BLOCK
        logits = jnp.einsum('bqhd,bkhd->bhqk', q[:, q0:end], k[:, :end]).astype(jnp.float32) * scale
        decay = c[:, :, q0:end, None] - c[:, :, None, :end]
        dist = (q0 + jnp.arange(Q_BLOCK))[:, None] - jnp.arange(end)[None, :]
        logits = jnp.where(dist >= 0, logits + decay, -jnp.inf)
        probs = jax.nn.softmax(logits, axis=-1)
        outs.append(jnp.einsum('bhqk,bkhd->bqhd', probs.astype(v.dtype), v[:, :end]))
    return jnp.concatenate(outs, axis=1).reshape(B, S, FOX_WIDTH)

def peer_ffn(h, w_query, sub_keys, expert_u, expert_v):
    B, S, D = h.shape
    T = B * S
    t = h.reshape(T, D)
    q = (t @ w_query).reshape(T, PEER_HEADS, 2, PEER_HALF)
    s = jnp.einsum('thpd,pnd->thpn', q, sub_keys).astype(jnp.float32)
    top_s, top_i = lax.top_k(s, PEER_TOPK)
    cand_s = (top_s[:, :, 0, :, None] + top_s[:, :, 1, None, :]).reshape(T, PEER_HEADS, PEER_TOPK * PEER_TOPK)
    cand_i = (top_i[:, :, 0, :, None] * N_KEYS + top_i[:, :, 1, None, :]).reshape(T, PEER_HEADS, PEER_TOPK * PEER_TOPK)
    best_s, best_pos = lax.top_k(cand_s, PEER_TOPK)
    experts = jnp.take_along_axis(cand_i, best_pos, axis=-1).reshape(T, PEER_HEADS * PEER_TOPK)
    gates = jax.nn.softmax(best_s, axis=-1).reshape(T, PEER_HEADS * PEER_TOPK)
    nblk = T // TOKEN_BLOCK

    def expert_block(args):
        tb, eb, gb = args
        act = jax.nn.gelu(jnp.einsum('td,ted->te', tb, expert_u[eb]).astype(jnp.float32), approximate=False)
        return jnp.einsum('te,ted->td', (gb * act).astype(tb.dtype), expert_v[eb])

    out = lax.map(expert_block, (t.reshape(nblk, TOKEN_BLOCK, D),
                                 experts.reshape(nblk, TOKEN_BLOCK, -1),
                                 gates.reshape(nblk, TOKEN_BLOCK, -1)))
    return out.reshape(B, S, D)

def first_inputs(seed: int = 0) -> dict:
    key = jax.random.key(seed)
    ks = jax.random.split(key, 17)
    nrm = lambda k, shape, scale: jax.random.normal(k, shape, jnp.float32) * scale
    return {
        "x": nrm(ks[0], (BATCH, SEQ, D_MODEL), 1.0),
        "norm1_g": 1.0 + nrm(ks[1], (DEPTH, D_MODEL), 0.02),
        "w_in": nrm(ks[2], (DEPTH, D_MODEL, IN_WIDTH), D_MODEL ** -0.5),
        "b_forget": 2.0 + nrm(ks[3], (DEPTH, N_FOX_HEADS), 0.1),
        "diff_lambda": nrm(ks[4], (DEPTH, 4, HEAD_DIM), 0.1),
        "diff_subln_g": 1.0 + nrm(ks[5], (DEPTH, DIFF_V_DIM), 0.02),
        "w_diff_o": nrm(ks[6], (DEPTH, DIFF_WIDTH, D_MODEL), DIFF_WIDTH ** -0.5),
        "w_fox_o": nrm(ks[7], (DEPTH, FOX_WIDTH, D_MODEL), FOX_WIDTH ** -0.5),
        "w_out": nrm(ks[8], (DEPTH, D_MODEL, D_MODEL), D_MODEL ** -0.5),
        "norm2_g": 1.0 + nrm(ks[9], (DEPTH, D_MODEL), 0.02),
        "w_query": nrm(ks[10], (DEPTH, D_MODEL, PEER_HEADS * PEER_QDIM), D_MODEL ** -0.5),
        "sub_keys": nrm(ks[11], (DEPTH, 2, N_KEYS, PEER_HALF), PEER_HALF ** -0.5),
        "expert_u": nrm(ks[12], (DEPTH, N_EXPERTS, D_MODEL), D_MODEL ** -0.5),
        "expert_v": nrm(ks[13], (DEPTH, N_EXPERTS, D_MODEL), (PEER_HEADS * PEER_TOPK) ** -0.5),
        "rel_bias": nrm(ks[14], (N_BUCKETS, N_DIFF_HEADS), 0.5),
        "final_norm_g": 1.0 + nrm(ks[15], (D_MODEL,), 0.02),
    }

def first_block(x, norm1_g, w_in, b_forget, diff_lambda, diff_subln_g, w_diff_o, w_fox_o, w_out,
              norm2_g, w_query, sub_keys, expert_u, expert_v, rel_bias, final_norm_g):
    B, S, D = x.shape
    split_points = np.cumsum(IN_SIZES)[:-1].tolist()
    for layer in range(DEPTH):
        lam_init = 0.8 - 0.6 * math.exp(-0.3 * layer)
        h = rms_norm(x, norm1_g[layer])
        proj = h @ w_in[layer]
        dq, dk, dv, fq, fk, fv, ff, ga, gb = jnp.split(proj, split_points, axis=-1)
        y_diff = diff_attention(dq.reshape(B, S, N_DIFF_HEADS, 2, HEAD_DIM),
                                dk.reshape(B, S, N_DIFF_HEADS, 2, HEAD_DIM),
                                dv.reshape(B, S, N_DIFF_HEADS, DIFF_V_DIM),
                                rel_bias, diff_lambda[layer], lam_init, diff_subln_g[layer])
        y_fox = forgetting_attention(fq.reshape(B, S, N_FOX_HEADS, HEAD_DIM),
                                     fk.reshape(B, S, N_FOX_HEADS, HEAD_DIM),
                                     fv.reshape(B, S, N_FOX_HEADS, HEAD_DIM),
                                     ff + b_forget[layer])
        merged = jax.nn.sigmoid(ga) * (y_diff @ w_diff_o[layer]) + jax.nn.sigmoid(gb) * (y_fox @ w_fox_o[layer])
        x = x + merged @ w_out[layer]
        x = x + peer_ffn(rms_norm(x, norm2_g[layer]), w_query[layer], sub_keys[layer],
                         expert_u[layer], expert_v[layer])
    return rms_norm(x, final_norm_g)


N_META = 16
BLOCK = 128
MLA_HEADS = 4
Q_LORA = 256
KV_LORA = 256
QK_NOPE = 128
QK_ROPE = 64
QK_HEAD = QK_NOPE + QK_ROPE
V_HEAD = 128
MLA_WIDTH = MLA_HEADS * V_HEAD
RET_HEADS = 4
RET_HEAD = 128
RET_WIDTH = RET_HEADS * RET_HEAD
MIX_WIDTH = MLA_WIDTH + RET_WIDTH
IN_SIZES_2 = (Q_LORA, KV_LORA, QK_ROPE, RET_WIDTH, RET_WIDTH, RET_WIDTH, RET_WIDTH)
N_IN = sum(IN_SIZES_2)
D_FF = -(-(8 * D_MODEL) // (3 * 256)) * 256
ROPE_BASE = 10000.0
NEG_INF = -1e30


def rms_norm_2(x, g):
    xf = x.astype(jnp.float32)
    y = xf * lax.rsqrt(jnp.mean(xf * xf, axis=-1, keepdims=True) + EPS)
    return (y * g.astype(jnp.float32)).astype(x.dtype)

def rope_tables(n_pos, dim):
    inv = ROPE_BASE ** (-jnp.arange(0, dim, 2, dtype=jnp.float32) / dim)
    ang = jnp.arange(n_pos, dtype=jnp.float32)[:, None] * inv[None, :]
    return jnp.cos(ang), jnp.sin(ang)

def apply_rope(x, cos, sin):
    x1, x2 = jnp.split(x, 2, axis=-1)
    c = cos[:, None, :].astype(x.dtype)
    s = sin[:, None, :].astype(x.dtype)
    return jnp.concatenate([x1 * c - x2 * s, x2 * c + x1 * s], axis=-1)

def mla_mixer(c_q, c_kv, k_pe, q_a_g, w_q_b, kv_a_g, w_kv_b, q_g, k_g, out_g, cos, sin):
    B, L, _ = c_q.shape
    q = (rms_norm_2(c_q, q_a_g) @ w_q_b).reshape(B, L, MLA_HEADS, QK_HEAD)
    kv = (rms_norm_2(c_kv, kv_a_g) @ w_kv_b).reshape(B, L, MLA_HEADS, QK_NOPE + V_HEAD)
    k_nope, v = kv[..., :QK_NOPE], kv[..., QK_NOPE:]
    k_pe_h = jnp.broadcast_to(k_pe[:, :, None, :], (B, L, MLA_HEADS, QK_ROPE))
    k = jnp.concatenate([k_nope, k_pe_h], axis=-1)
    q = rms_norm_2(q, q_g)
    k = rms_norm_2(k, k_g)
    q = jnp.concatenate([q[..., :QK_NOPE], apply_rope(q[..., QK_NOPE:], cos, sin)], axis=-1)
    k = jnp.concatenate([k[..., :QK_NOPE], apply_rope(k[..., QK_NOPE:], cos, sin)], axis=-1)
    scale = QK_HEAD ** -0.5
    bounds = [0] + [N_META + BLOCK * j for j in range((L - N_META) // BLOCK + 1)]
    outs = []
    for start, end in zip(bounds[:-1], bounds[1:]):
        qb, kb, vb = q[:, start:end], k[:, :end], v[:, :end]
        s = jnp.einsum('bqhd,bkhd->bhqk', qb, kb).astype(jnp.float32) * scale
        causal = jnp.arange(start, end)[:, None] >= jnp.arange(end)[None, :]
        s = jnp.where(causal[None, None], s, NEG_INF)
        p = jax.nn.softmax(s, axis=-1).astype(vb.dtype)
        outs.append(jnp.einsum('bhqk,bkhd->bqhd', p, vb))
    o = jnp.concatenate(outs, axis=1)
    o = rms_norm_2(o, out_g.reshape(MLA_HEADS, V_HEAD))
    return o.reshape(B, L, MLA_WIDTH)

def retention_mixer(rq, rk, rv, rg, norm_g, norm_b, cos, sin):
    B, L, _ = rq.shape
    dt = rq.dtype
    q = apply_rope(rq.reshape(B, L, RET_HEADS, RET_HEAD), cos, sin).astype(jnp.float32)
    k = (apply_rope(rk.reshape(B, L, RET_HEADS, RET_HEAD), cos, sin) * RET_HEAD ** -0.5).astype(jnp.float32)
    v = rv.reshape(B, L, RET_HEADS, RET_HEAD).astype(jnp.float32)
    pad = BLOCK - N_META
    padw = ((0, 0), (pad, 0), (0, 0), (0, 0))
    q, k, v = (jnp.pad(t, padw) for t in (q, k, v))
    Lp = L + pad
    n_chunks = Lp // BLOCK

    def to_chunks(t):
        return t.reshape(B, n_chunks, BLOCK, RET_HEADS, RET_HEAD).transpose(1, 0, 3, 2, 4)

    qc, kc, vc = to_chunks(q), to_chunks(k), to_chunks(v)
    gamma = 1.0 - 2.0 ** (-5.0 - jnp.arange(RET_HEADS, dtype=jnp.float32))
    log_g = jnp.log(gamma)
    idx = jnp.arange(BLOCK, dtype=jnp.float32)
    diff = idx[:, None] - idx[None, :]
    decay = jnp.where(diff >= 0, jnp.exp(jnp.maximum(diff, 0.0)[None] * log_g[:, None, None]), 0.0)
    xi = jnp.exp((idx + 1.0)[None, :] * log_g[:, None])
    zeta = jnp.exp((BLOCK - 1.0 - idx)[None, :] * log_g[:, None])
    chunk_decay = jnp.exp(BLOCK * log_g)

    def step(state, inp):
        qb, kb, vb = inp
        s = jnp.einsum('bhnd,bhmd->bhnm', qb, kb) * decay[None]
        inner = jnp.einsum('bhnm,bhmd->bhnd', s, vb)
        cross = jnp.einsum('bhnd,bhde->bhne', qb, state) * xi[None, :, :, None]
        new_state = state * chunk_decay[None, :, None, None] + jnp.einsum(
            'bhmd,bhme->bhde', kb * zeta[None, :, :, None], vb)
        return new_state, inner + cross

    state0 = jnp.zeros((B, RET_HEADS, RET_HEAD, RET_HEAD), jnp.float32)
    _, o = lax.scan(step, state0, (qc, kc, vc))
    o = o.transpose(1, 0, 3, 2, 4).reshape(B, Lp, RET_HEADS, RET_HEAD)[:, pad:]
    mu = jnp.mean(o, axis=-1, keepdims=True)
    var = jnp.mean(jnp.square(o - mu), axis=-1, keepdims=True)
    o = ((o - mu) * lax.rsqrt(var + EPS)).reshape(B, L, RET_WIDTH)
    o = o * norm_g.astype(jnp.float32) + norm_b.astype(jnp.float32)
    return (jax.nn.silu(rg.astype(jnp.float32)) * o).astype(dt)

def second_inputs(seed: int = 0) -> dict:
    key = jax.random.key(seed)
    ks = jax.random.split(key, 20)

    def w(k, shape, fan_in):
        return jax.random.normal(k, shape, jnp.float32) * fan_in ** -0.5

    def gain(k, shape):
        return 1.0 + 0.02 * jax.random.normal(k, shape, jnp.float32)

    return {
        "x": jax.random.normal(ks[0], (BATCH, SEQ, D_MODEL), jnp.float32),
        "meta_tokens": jax.random.normal(ks[1], (N_META, D_MODEL), jnp.float32),
        "attn_norm_g": gain(ks[2], (DEPTH, D_MODEL)),
        "w_in": w(ks[3], (DEPTH, D_MODEL, N_IN), D_MODEL),
        "q_a_norm_g": gain(ks[4], (DEPTH, Q_LORA)),
        "w_q_b": w(ks[5], (DEPTH, Q_LORA, MLA_HEADS * QK_HEAD), Q_LORA),
        "kv_a_norm_g": gain(ks[6], (DEPTH, KV_LORA)),
        "w_kv_b": w(ks[7], (DEPTH, KV_LORA, MLA_HEADS * (QK_NOPE + V_HEAD)), KV_LORA),
        "q_norm_g": gain(ks[8], (DEPTH, QK_HEAD)),
        "k_norm_g": gain(ks[9], (DEPTH, QK_HEAD)),
        "mla_out_norm_g": gain(ks[10], (DEPTH, MLA_WIDTH)),
        "ret_norm_g": gain(ks[11], (DEPTH, RET_WIDTH)),
        "ret_norm_b": 0.02 * jax.random.normal(ks[12], (DEPTH, RET_WIDTH), jnp.float32),
        "w_out": w(ks[13], (DEPTH, MIX_WIDTH, D_MODEL), MIX_WIDTH),
        "ffn_norm_g": gain(ks[14], (DEPTH, D_MODEL)),
        "w_gate_up": w(ks[15], (DEPTH, D_MODEL, 2 * D_FF), D_MODEL),
        "w_down": w(ks[16], (DEPTH, D_FF, D_MODEL), D_FF),
    }

def second_block(x, meta_tokens, attn_norm_g, w_in, q_a_norm_g, w_q_b, kv_a_norm_g, w_kv_b,
              q_norm_g, k_norm_g, mla_out_norm_g, ret_norm_g, ret_norm_b, w_out,
              ffn_norm_g, w_gate_up, w_down):
    B = x.shape[0]
    meta = jnp.broadcast_to(meta_tokens[None].astype(x.dtype), (B, N_META, D_MODEL))
    h_res = jnp.concatenate([meta, x], axis=1)
    L = h_res.shape[1]
    cos_m, sin_m = rope_tables(L, QK_ROPE)
    cos_r, sin_r = rope_tables(L, RET_HEAD)
    split_idx = [int(v) for v in np.cumsum(IN_SIZES_2)[:-1]]
    for l in range(DEPTH):
        h = rms_norm_2(h_res, attn_norm_g[l])
        z = h @ w_in[l]
        c_q, c_kv, k_pe, rq, rk, rv, rg = jnp.split(z, split_idx, axis=-1)
        y_mla = mla_mixer(c_q, c_kv, k_pe, q_a_norm_g[l], w_q_b[l], kv_a_norm_g[l], w_kv_b[l],
                          q_norm_g[l], k_norm_g[l], mla_out_norm_g[l], cos_m, sin_m)
        y_ret = retention_mixer(rq, rk, rv, rg, ret_norm_g[l], ret_norm_b[l], cos_r, sin_r)
        y = jnp.concatenate([y_mla, y_ret], axis=-1) @ w_out[l]
        h_res = h_res + y
        hf = rms_norm_2(h_res, ffn_norm_g[l])
        gate, up = jnp.split(hf @ w_gate_up[l], 2, axis=-1)
        h_res = h_res + (jax.nn.silu(gate) * up) @ w_down[l]
    return h_res[:, N_META:]


def setup_inputs(seed=0):
    out = dict(first_inputs(seed))
    for name, value in second_inputs(seed + 1).items():
        if name != "x":
            out[name + "_2"] = value
    return out


def reference(
    x, norm1_g, w_in, b_forget, diff_lambda, diff_subln_g, w_diff_o, w_fox_o, w_out, norm2_g,
    w_query, sub_keys, expert_u, expert_v, rel_bias, final_norm_g, meta_tokens_2, attn_norm_g_2,
    w_in_2, q_a_norm_g_2, w_q_b_2, kv_a_norm_g_2, w_kv_b_2, q_norm_g_2, k_norm_g_2,
    mla_out_norm_g_2, ret_norm_g_2, ret_norm_b_2, w_out_2, ffn_norm_g_2, w_gate_up_2, w_down_2,
):
    x = first_block(
        x, norm1_g, w_in, b_forget, diff_lambda, diff_subln_g, w_diff_o, w_fox_o, w_out,
        norm2_g, w_query, sub_keys, expert_u, expert_v, rel_bias, final_norm_g,
    )
    return second_block(
        x, meta_tokens_2, attn_norm_g_2, w_in_2, q_a_norm_g_2, w_q_b_2, kv_a_norm_g_2, w_kv_b_2,
        q_norm_g_2, k_norm_g_2, mla_out_norm_g_2, ret_norm_g_2, ret_norm_b_2, w_out_2,
        ffn_norm_g_2, w_gate_up_2, w_down_2,
    )


_drawn_inputs = setup_inputs


def setup_inputs(seed=0):
    import zlib

    import numpy as np

    out = dict(_drawn_inputs(seed))
    spreads = {}
    factors = {'norm2_g': 4.837,
     'q_a_norm_g_2': 6.656,
     'kv_a_norm_g_2': 2.85,
     'q_norm_g_2': 6.089,
     'k_norm_g_2': 6.881,
     'mla_out_norm_g_2': 3.222,
     'ret_norm_g_2': 5.749,
     'ret_norm_b_2': 5.63,
     'ffn_norm_g_2': 3.385}
    for name, (base, spread) in spreads.items():
        noise = np.random.default_rng([zlib.crc32(name.encode()), seed]).standard_normal(out[name].shape)
        drawn = base * np.exp(spread * noise) if base else spread * noise
        out[name] = __import__('jax').numpy.asarray(drawn.astype(out[name].dtype))
    for name, factor in factors.items():
        out[name] = (out[name] * factor).astype(out[name].dtype)
    return out
```

```python
import math
from contextlib import ExitStack

import numpy as np
import concourse.bass as bass
from concourse import mybir

ALU = mybir.AluOpType
ACT = mybir.ActivationFunctionType
AX = mybir.AxisListType
F32 = mybir.dt.float32
U32 = mybir.dt.uint32

P = 128
D = 1024
KC = D // P
SEQ = 256
META = 16
T2 = SEQ + META
DEPTH = 2
EPS = 1e-6
NEG = -1e30
BIG = 3e38

DH = 4
FH = 8
MAPS = 2 * DH + FH
BUCKETS = 32
MAX_DIST = 128
PH = 8
TOPK = 16
NEXP = 128 * 128
SLOTS = PH * TOPK
RANKS = [(0, 1, 16), (1, 1, 8), (2, 1, 5), (3, 1, 4), (4, 1, 3), (5, 3, 2), (8, 8, 1)]
CAND = sum(n * m for _, n, m in RANKS)

MH = 4
RH = 4
QKH = 192
DFF = 2816
FC = DFF // P
TILE = 4096
RING = 3
TILES1 = 18
TILES2 = 27
GB = 4
UB = 2 * GB
BANKS = 4

C1_N1, C1_N2, C1_SUB, C1_LAM, C1_BF, C1_LI, C1_FF, C1_KEY = 0, 8, 16, 17, 273, 274, 276, 340
NC1 = 596
C2_N1, C2_N2, C2_QA, C2_KVA, C2_QG, C2_KG, C2_MO, C2_RG, C2_RB, C2_KPE = 0, 8, 16, 18, 20, 22, 24, 28, 32, 36
NC2 = C2_KPE + KC * 64
K_ID, K_FLIP, K_CEN, K_PM, K_PR, K_MASK, K_IOTA, K_OH = 0, 128, 256, 384, 512, 576, 960, 1010
NK1 = K_OH + 384
K2_D, K2_CR, K2_SR, K2_CM, K2_SM, K2_MASK = 0, 1728, 2000, 2272, 2544, 2816
NK2 = K2_MASK + T2

PLAN = {
    1: (["norm1"] + [f"dq{c}" for c in range(4)] + [f"dk{c}" for c in range(4)] + ["dv0", "dv1"]
        + [f"fq{c}" for c in range(4)] + [f"fk{c}" for c in range(4)] + ["fv0", "fv1", "ff"]
        + [f"gate{c}" for c in range(16)] + [f"dnorm{h}" for h in range(DH)]
        + [f"do{c}" for c in range(8)] + [f"fo{c}" for c in range(8)] + [f"out{c}" for c in range(8)]
        + ["norm2"] + [f"hn{c}" for c in range(4)] + [f"wq{c}" for c in range(16)]
        + [f"s{c}" for c in range(8)] + [f"ft{c}" for c in range(4)]),
    "f": ["normf"],
    2: (["norm1", "cq0", "cq1", "cq2", "cq3", "kpe"] + [f"rq{c}" for c in range(4)] + ["qa", "kva", "kperm"]
        + [f"rk{c}" for c in range(4)] + [f"rv{c}" for c in range(3)] + [f"rg{c}" for c in range(4)]
        + [f"qn{c}" for c in range(4)] + [f"qr{c}" for c in range(4)] + [f"kn{c}" for c in range(4)]
        + [f"v{c}" for c in range(3)] + [f"rqp{c}" for c in range(4)] + [f"rkp{c}" for c in range(4)]
        + [f"qs{c}" for c in range(4)] + [f"ks{c}" for c in range(4)] + [f"qp{c}" for c in range(4)]
        + [f"rc{c}" for c in range(4)] + [f"rs{c}" for c in range(4)] + [f"ms{c}" for c in range(4)]
        + [f"out{c}" for c in range(8)] + ["norm2"]
        + [f"{x}{2 * j + i}" for j in range(11) for x in "gu" for i in range(2)]
        + [f"dn{c}" for c in range(8)]),
}
GI = {b: {n: i for i, n in enumerate(p)} for b, p in PLAN.items()}
TURNS = {b: -(-len(p) // BANKS) * BANKS for b, p in PLAN.items()}

UNIT = {2 * h + 1: h for h in range(DH)} | {2 * DH + h: DH + h for h in range(FH)}

COUNTS = {
    "w_free": (RING, TILES1, 0, TILES2), "pj_full": (0, TURNS[1], TURNS["f"], TURNS[2]),
    "s_full": (0, MAPS, 0, RH + 2 * MH), "t_done": (0, DH + FH, 0, MH), "o_full": (0, DH + FH, 0, RH + MH),
    "v_free": (UB, 2 * SLOTS, 0, 0), "f_full": (0, 2, 0, 0),
    "evac": (BANKS, TURNS[1], TURNS["f"], TURNS[2]), "sq_done": (0, 3, 1, 15),
    "e_done": (0, 2 * MAPS, 0, 3 * MH), "pt_read": (1, DH + FH, 0, MH), "o_read": (1, DH + FH, 0, RH + MH),
    "act_misc": (0, 5, 0, 0), "gelu_done": (0, 2 * SLOTS // GB, 0, 0), "f_read": (0, 4, 0, 0),
    "h_done": (0, 2 * KC, 0, 2 * KC), "s_read": (2, MAPS, 0, RH + 2 * MH), "p_done": (0, MAPS, 0, MH),
    "dve_misc": (0, 160, 3, 62), "x_done": (1, KC + 4, KC, 2 * KC), "y_done": (0, DH + 8, 0, 8),
    "l_done": (0, 1, 0, 0), "c_done": (0, 1, 0, 0), "z_done": (0, 1, 0, 0), "gmax": (0, 2, 0, 0),
    "idx_a": (0, 10, 0, 0), "idx_b": (0, 8, 0, 0), "u_free": (UB, 2 * SLOTS, 0, 0),
    "diag_done": (1, 2 * SLOTS, 0, 0),
    "small_done": (0, 0, 0, 11), "rot_done": (0, 0, 0, 2 * RH + 2 * MH), "b2_act": (0, 0, 0, FC),
    "rstd": (0, 2 + DH, 1, 20),
    "cols_full": (0, 16, 0, 16),
}


def program(nc, x_in, meta_in, ws, c1_in, c2_in, fin_g, rel, k1_in, k2_in, eu, ev, out):
    with ExitStack() as ctx:
        def sb(name, shape, dt=F32):
            return ctx.enter_context(nc.sbuf_tensor(name, shape, dt))

        def bank(name):
            return ctx.enter_context(nc.psum_tensor(name, [P, 512], F32))

        def sem(name):
            return ctx.enter_context(nc.semaphore(name))

        wring = sb("wring", [P, RING, TILE])
        area = sb("area", [P, 16384])
        area2 = sb("area2", [P, 10752])
        xT = sb("xT", [P, KC, T2])
        hT = sb("hT", [P, KC, T2])
        sq = sb("sq", [P, KC, T2])
        ms = sb("ms", [P, 4, T2])

        rstd = sb("rstd", [P, 8, T2])
        cols = sb("cols", [P, max(NC1, NC2)])
        fing = sb("fing", [P, KC])
        relb = sb("relb", [BUCKETS, DH])
        kst = sb("kst", [P, K_OH])
        ones = sb("ones", [P, P])
        eps = sb("eps", [P, 4])
        nsel = sb("nsel", [FH, FH])
        bias = sb("bias", [P, DH, 384])
        nmax = sb("nmax", [P, 2, 3])
        esum = sb("esum", [P, 2, 3])
        erec = sb("erec", [P, 2, 3])
        lam = sb("lam", [P, 8])
        loff = sb("loff", [P, 1])
        junk = sb("junk", [P, 64])
        zjunk = sb("zjunk", [P, 64])
        k2st = area[:, 16384 - NK2:16384]

        def part(buf, at, *shape):
            n = math.prod(shape)
            v = buf[:, at:at + n]
            names = "abc"[:len(shape)]
            if len(shape) == 1:
                return v
            return v.rearrange(f"p ({' '.join(names)}) -> p {' '.join(names)}",
                               **{k: s for k, s in zip(names, shape)})

        ident = kst[:, K_ID:K_ID + P]
        flip = kst[:, K_FLIP:K_FLIP + P]
        center = kst[:, K_CEN:K_CEN + P]
        swap128 = kst[:, K_PM:K_PM + P]
        swap64 = kst[0:64, K_PR:K_PR + 64]
        mask = kst[:, K_MASK:K_MASK + 384]
        iota = kst[:, K_IOTA:K_IOTA + CAND]

        dqT, dkT, fqT, fkT = (part(area, 1024 * i, 4, SEQ) for i in range(4))
        dv, fv = (part(area, 4096 + 1024 * i, 2, 512) for i in range(2))
        gate = part(area, 6144, 16, SEQ)
        doT, foT = part(area, 10240, 8, SEQ), part(area, 12288, 8, SEQ)
        ydT, yfT = part(area, 14336, 4, SEQ), part(area, 15360, 4, SEQ)
        urow, vrow = part(area, 0, UB, D), part(area, UB * D, UB, D)
        mgT = part(area2, 0, 8, SEQ)
        qT = part(area2, 0, 16, SEQ)
        sc = part(area2, 4096, 16, P)
        h2n = part(area2, 6144, 2, D)
        oTmp = part(area2, 8192, 8, SEQ)
        eq = part(area2, 8192, 32, CAND)
        cnd = part(area2, 9792, PH, CAND)
        cidx = part(area2, 10192, PH, CAND)
        gates = sb("gates", [P, PH, TOPK])
        gsum = sb("gsum", [P, 2, PH])
        idxf = sb("idxf", [P, SLOTS + TOPK])
        idx = sb("idx", [P, 2 * TOPK], U32)
        dots = sb("dots", [P, 2, GB])
        gl = sb("gl", [P, 2, GB])
        wgt = sb("wgt", [P, 2, GB])
        hflat = hT[:, :, :].rearrange("p c t -> p (c t)")
        diag = part(hflat, 0, UB, P)
        topv, topf = part(hflat, 1024, 16, TOPK), part(hflat, 1280, 16, TOPK)
        bestv, bestf = part(hflat, 1792, PH, TOPK), part(hflat, 1920, PH, TOPK)
        bestp = hflat[:, 2048:2176].bitcast(U32).rearrange("p (a k) -> p a k", k=TOPK)
        topi = hflat[:, 1536:1792].bitcast(U32).rearrange("p (a k) -> p a k", k=TOPK)
        fn = part(area2, 0, D)
        fT = part(area2, D, 8, P)
        sc1 = sq[:, :, :].rearrange("p c t -> p (c t)")[:, 0:2048].rearrange("p (a n) -> p a n", n=P)

        half = eps[:, 2:3]
        zeros = eps[:, 3:4].to_broadcast([P, 512])
        nl, ex, pr, pt = (part(area2, 4352 + 1312 * i, 2, n) for i, n in enumerate((656, 656, 656, 432)))
        fox = area2[0:FH, 9152:9152 + 6 * SEQ].rearrange("p (a n) -> p a n", a=6)
        onehot = area[0:BUCKETS, 0:384]
        gvec = area2[0:DH, 0:384]
        cosR, sinR = (k2st[:, c:c + T2] for c in (K2_CR, K2_SR))
        cosM, sinM = (k2st[0:64, c:c + T2] for c in (K2_CM, K2_SM))

        cq = part(area, 0, 4, T2)
        kpe, kpg, kro = (part(area, 1088 + T2 * i, T2) for i in range(3))
        rq, rk = part(area, 1904, 4, T2), part(area, 2992, 4, T2)
        rv, v2 = part(area, 4080, 3, 512), part(area, 11056, 3, 512)
        rgt, rgr = part(area, 5616, 4, T2), part(area, 6704, 4, T2)
        qn, qr, kn = (part(area, 7792 + 1088 * i, 4, T2) for i in range(3))
        kr, ro, mo = rk, rq, qn
        yT, tmpR = part(area2, 0, 8, T2), part(area2, 0, 8, T2)
        tmpP = part(area2, 2176, 5, T2)
        actT = part(area2, 4352, FC, T2)
        oTmp2 = part(area, 0, 8, T2)
        gbuf = part(area, 4352, 2, 6, T2)

        PJ = [bank(f"pj{i}") for i in range(BANKS)]
        S = [bank("s0"), bank("s1")]
        PT = bank("ptb")
        O = bank("ob")

        N = {n: sem(n) for n in COUNTS}
        w_full = [sem(f"w_full{i}") for i in range(RING)]
        u_full = [sem(f"u_full{i}") for i in range(UB)]
        v_full = [sem(f"v_full{i}") for i in range(UB)]
        const_full, const2_full = sem("const_full"), sem("const2_full")
        memset_done, setup_dve = sem("memset_done"), sem("setup_dve")
        setup_pe, setup_act = sem("setup_pe"), sem("setup_act")
        scratch_out, scratch_in, out_full = sem("scratch_out"), sem("scratch_in"), sem("out_full")
        held = {e: sem(f"held_{e}") for e in ("pe", "act", "dve", "pool")}

        class Layer:

            def __init__(self, block, l):
                self.block, self.l, self.n = block, l, {}
                self.g = 0

            def at(self, name, k):
                pre, a, f, b = COUNTS[name]
                if self.block == 1:
                    return self.l * a + (pre + k)
                if self.block == "f":
                    return pre + DEPTH * a + k
                return self.l * b + (pre + DEPTH * a + f + k)

            def inc(self, ins, name, by=1):
                ins.then_inc(N[name], by)
                self.n[name] = self.n.get(name, 0) + by

            def wait(self, eng, name, k):
                eng.wait_ge(N[name], self.at(name, k))

            def hold(self, eng, who, name, k):
                eng.wait_ge(N[name], self.at(name, k))
                eng.sem_inc(held[who], 1)

            def evacuated(self, eng, group):
                self.wait(eng, "evac", GI[self.block][group] + 1)

            def check(self, names):
                i = {1: 1, "f": 2, 2: 3}[self.block]
                for n in names:
                    if self.n.get(n, 0) != COUNTS[n][i]:
                        print("COUNT", self.block, n, self.n.get(n, 0), "declared", COUNTS[n][i])
                        assert False, n

        scratch = nc.dram_tensor("bias_scratch", [DH, 384], F32, kind="Internal")
        block = ctx.enter_context(nc.Block())

        @block.sync
        def _(sp):
            sp.dma_start(kst[:], k1_in[:, 0:K_OH]).then_inc(const_full, 16)
            sp.dma_start(onehot, k1_in[0:BUCKETS, K_OH:NK1]).then_inc(const_full, 16)
            sp.dma_start(relb[:], rel).then_inc(const_full, 16)
            sp.dma_start(xT[:, :, META:T2], x_in).then_inc(const_full, 16)
            sp.dma_start(xT[:, :, 0:META], meta_in).then_inc(const_full, 16)
            sp.dma_start(fing[:], fin_g).then_inc(const_full, 16)
            with sp.Fori(0, DEPTH * (TILES1 + TILES2) // RING) as r:
                for i in range(RING):
                    sp.wait_ge(N["w_free"], r * RING + (i + 1))
                    sp.dma_start(wring[:, i, :], ws[r * RING + i, :, :]).then_inc(w_full[i], 16)
            sp.wait_ge(N["x_done"], COUNTS["x_done"][0] + DEPTH * (COUNTS["x_done"][1] + COUNTS["x_done"][3]) + COUNTS["x_done"][2])
            sp.dma_start(out, xT[:, :, META:T2]).then_inc(out_full, 16)
            sp.wait_ge(out_full, 16)

        def tile_ready(eng, L, t):
            if L.block == 1:
                eng.wait_ge(w_full[t % RING], L.l * (16 * TILES1 // RING) + 16 * (t // RING + 1))
            else:
                eng.wait_ge(w_full[t % RING], L.l * (16 * TILES2 // RING)
                            + 16 * (DEPTH * TILES1 // RING + t // RING + 1))
            return wring[:, t % RING, :]

        TX = slice(META, T2)
        ATILES = ((0, P), (P, P), (2 * P, T2 - 2 * P))

        @block.tensor
        def _(pe):
            pe.sem_inc(N["w_free"], RING)
            pe.sem_inc(N["v_free"], UB)
            pe.wait_ge(const_full, 96)
            pe.matmul(PJ[0][0:DH, 0:384], relb[:], onehot,
                      start=True, stop=True).then_inc(setup_pe, 1)
            pe.wait_ge(scratch_in, 16)
            pe.wait_ge(setup_act, 1)
            for h in range(DH):
                m = pe.matmul(PJ[h][:, 0:256], flip, doT[:, h, :], start=True, stop=True)
            m.then_inc(setup_pe, 1)
            pe.wait_ge(setup_dve, 1)
            pe.wait_ge(memset_done, 1)

            class Products(Layer):
                owed = False

                def mm(self, out, lhs, rhs, start, stop, last=False):
                    m = pe.matmul(out, lhs, rhs, start=start, stop=stop)
                    if self.owed and not last:
                        self.inc(m, "w_free")
                        self.owed = False
                    return m

                def group(self, name):
                    assert PLAN[self.block][self.g] == name, (PLAN[self.block][self.g], name)
                    self.wait(pe, "evac", self.g + 1 - BANKS)
                    b = PJ[self.g % BANKS]
                    self.g += 1
                    return b

                def stats(self, name, squares, n):
                    b = self.group(name)
                    for c, s in enumerate(squares):
                        m = self.mm(b[:, 0:n], ones[0:s.shape[0], :], s, c == 0, c == len(squares) - 1,
                                    last=c == len(squares) - 1)
                    self.inc(m, "pj_full")

                def chunk(self, name, w, m0, rhs, kcs, n, m=P):
                    b = self.group(name)
                    for k in range(kcs):
                        i = self.mm(b[0:m, 0:n], w[:, k, m0:m0 + m], rhs(k), k == 0, k == kcs - 1, last=k == kcs - 1)
                    self.inc(i, "pj_full")

                def tokens(self, name, w, n0, act, kcs, t0, m):
                    b = self.group(name)
                    for k in range(kcs):
                        i = self.mm(b[0:m, :], act(k)[:, t0:t0 + m], w[:, k, n0:n0 + 512], k == 0, k == kcs - 1,
                                    last=k == kcs - 1)
                    self.inc(i, "pj_full")

                def pad(self):
                    n = TURNS[self.block] - len(PLAN[self.block])
                    assert self.g == len(PLAN[self.block]) and not self.owed
                    if n:
                        self.wait(pe, "pj_full", self.n["pj_full"])
                        pe.sem_inc(N["pj_full"], n)
                        self.n["pj_full"] += n

            def block1(l):
                L = Products(1, l)
                keys = cols[:, C1_KEY:C1_KEY + 256].rearrange("p (a n) -> p a n", a=2)
                hx = lambda k: hT[:, k, TX]

                def feature_tile(t, names):
                    w = tile_ready(pe, L, t).rearrange("p (k n) -> p k n", k=KC)
                    for m, n in enumerate(names):
                        L.chunk(n, w, m * P, hx, KC, SEQ)
                    L.owed = True

                def token_tile(t, name):
                    w = tile_ready(pe, L, t).rearrange("p (k n) -> p k n", k=KC)
                    for tt in range(2):
                        L.tokens(f"{name}{tt}", w, 0, lambda k: hT[:, k, :], KC, META + tt * P, P)
                    L.owed = True

                L.wait(pe, "sq_done", 1)
                L.stats("norm1", [sq[:, c, TX] for c in range(KC)], SEQ)
                L.wait(pe, "h_done", KC)
                feature_tile(0, [f"dq{c}" for c in range(4)])
                feature_tile(1, [f"dk{c}" for c in range(4)])
                token_tile(2, "dv")
                feature_tile(3, [f"fq{c}" for c in range(4)])
                feature_tile(4, [f"fk{c}" for c in range(4)])
                token_tile(5, "fv")
                L.wait(pe, "cols_full", 16)
                L.chunk("ff", cols[:, C1_FF:C1_FF + KC * FH].rearrange("p (k n) -> p k n", k=KC), 0, hx, KC, SEQ, m=FH)

                def scores(i):
                    fo = i >= 2 * DH
                    if i == 0:
                        L.evacuated(pe, "dk3")
                    if i == 2 * DH:
                        L.evacuated(pe, "fk3")
                        L.wait(pe, "c_done", 1)
                    L.wait(pe, "s_read", i - 1)
                    j = i - 2 * DH if fo else i
                    q, k = (fqT, fkT) if fo else (dqT, dkT)
                    r = slice(64 * (j % 2), 64 * (j % 2) + 64)
                    for qt, (c0, n) in enumerate(((0, P), (P, 2 * P))):
                        o = S[i % 2][:, c0:c0 + n]
                        m = pe.matmul(o, q[r, j // 2, qt * P:(qt + 1) * P], k[r, j // 2, 0:n], start=True, stop=not fo)
                        if fo:
                            pe.matmul(o, fox[:, 5, qt * P:(qt + 1) * P], ident[0:FH, j:j + 1].to_broadcast([FH, n]), start=False, stop=False)
                            m = pe.matmul(o, nsel[:, j:j + 1].to_broadcast([FH, P]), fox[:, 5, 0:n], start=False, stop=True)
                    L.inc(m, "s_full")

                def turn(u, i):
                    L.wait(pe, "p_done", i + 1)
                    L.wait(pe, "pt_read", u)
                    for c in range(3):
                        m = pe.transpose(PT[:, c * P:(c + 1) * P], pr[:, u % 2, c * P:(c + 1) * P], ident)
                    L.inc(m, "t_done")

                def values(u):
                    if u == 0:
                        L.evacuated(pe, "fv1")
                    L.wait(pe, "pt_read", u + 1)
                    L.wait(pe, "o_read", u)
                    v, c = (dv, u) if u < DH else (fv, (u - DH) // 2)
                    pe.matmul(O[:, 0:SEQ], v[:, 0, c * P:(c + 1) * P], pt[:, u % 2, 0:SEQ], start=True, stop=False)
                    m = pe.matmul(O[:, P:SEQ], v[:, 1, c * P:(c + 1) * P], pt[:, u % 2, SEQ:384], start=False, stop=True)
                    L.inc(m, "o_full")

                for i in range(MAPS + 2):
                    if i < MAPS:
                        scores(i)
                        if i % 4 == 0:
                            w = tile_ready(pe, L, 6 + i // 4).rearrange("p (k n) -> p k n", k=KC)
                        L.chunk(f"gate{i}", w, (i % 4) * P, hx, KC, SEQ)
                        if i % 4 == 3:
                            L.owed = True
                    if i - 1 in UNIT:
                        turn(UNIT[i - 1], i - 1)
                    if i - 2 in UNIT:
                        values(UNIT[i - 2])

                L.wait(pe, "sq_done", 2)
                for h in range(DH):
                    L.stats(f"dnorm{h}", [sq[:, h, TX]], SEQ)
                w = tile_ready(pe, L, 10).rearrange("p (k n) -> p k n", k=4)
                L.wait(pe, "y_done", DH)
                for c in range(8):
                    L.chunk(f"do{c}", w, c * P, lambda k: ydT[:, k, :], 4, SEQ)
                L.owed = True
                w = tile_ready(pe, L, 11).rearrange("p (k n) -> p k n", k=4)
                L.wait(pe, "o_read", DH + FH)
                for c in range(8):
                    L.chunk(f"fo{c}", w, c * P, lambda k: yfT[:, k, :], 4, SEQ)
                L.owed = True
                L.wait(pe, "y_done", DH + 8)
                for t in range(2):
                    w = tile_ready(pe, L, 12 + t).rearrange("p (k n) -> p k n", k=KC)
                    for c in range(4):
                        L.chunk(f"out{4 * t + c}", w, c * P, lambda k: mgT[:, k, :], KC, SEQ)
                    L.owed = True

                L.wait(pe, "sq_done", 3)
                L.stats("norm2", [sq[:, c, TX] for c in range(KC)], SEQ)
                L.wait(pe, "h_done", 2 * KC)
                for tt in range(2):
                    for hf in range(2):
                        b = L.group(f"hn{2 * tt + hf}")
                        for c in range(4):
                            m = pe.transpose(b[:, c * P:(c + 1) * P],
                                             hT[:, 4 * hf + c, META + tt * P:META + (tt + 1) * P], ident)
                        L.inc(m, "pj_full")
                for t in range(4):
                    feature_tile(14 + t, [f"wq{4 * t + c}" for c in range(4)])
                L.evacuated(pe, "wq15")
                for tt in range(2):
                    for g in range(4):
                        b = L.group(f"s{4 * tt + g}")
                        for c in range(4):
                            hp = 4 * g + c
                            m = L.mm(b[:, c * P:(c + 1) * P], qT[:, hp, tt * P:(tt + 1) * P], keys[:, hp % 2, :],
                                     True, True, last=c == 3)
                        L.inc(m, "pj_full")
                for tt in range(2):
                    if tt:
                        L.wait(pe, "f_read", 2)
                    for n in range(2):
                        pe.matmul(S[n][:], ident, zeros, start=True, stop=False)
                    with pe.Fori(0, SLOTS // (8 * GB)) as j:
                        for g in range(8):
                            for i in range(GB):
                                b = GB * (g % 2) + i
                                pe.wait_ge(N["diag_done"], L.at("diag_done", tt * SLOTS + GB * g + i + 1) + j * (8 * GB))
                                pe.wait_ge(v_full[b], L.l * (32 * SLOTS // UB) + j * 64
                                           + 16 * (tt * SLOTS // UB + g // 2 + 1))
                                for n in range(2):
                                    m = pe.matmul(S[n][:], diag[:, b, :], vrow[:, b, n * 512:(n + 1) * 512],
                                                  start=False, stop=False)
                                m.then_inc(N["v_free"], 1)
                    L.n["v_free"] = L.n.get("v_free", 0) + SLOTS
                    for n in range(2):
                        m = pe.matmul(S[n][:], ident, zeros, start=False, stop=True)
                    L.inc(m, "f_full")
                    L.wait(pe, "f_read", 2 * tt + 2)
                    for hf in range(2):
                        b = L.group(f"ft{2 * tt + hf}")
                        for c in range(4):
                            m = pe.transpose(b[:, c * P:(c + 1) * P], fn[:, (4 * hf + c) * P:(4 * hf + c + 1) * P], ident)
                        L.inc(m, "pj_full")
                L.pad()
                L.check(["pj_full", "w_free", "s_full", "t_done", "o_full", "v_free", "f_full"])

            def block2(l):
                L = Products(2, l)
                hx = lambda k: hT[:, k, :]

                def feature_tile(t, names):
                    w = tile_ready(pe, L, t).rearrange("p (k n) -> p k n", k=KC)
                    for m, n in enumerate(names):
                        L.chunk(n, w, m * P, hx, KC, T2)
                    L.owed = True

                L.wait(pe, "sq_done", 1)
                L.stats("norm1", [sq[:, c, :] for c in range(KC)], T2)
                L.wait(pe, "h_done", KC)
                feature_tile(0, [f"cq{c}" for c in range(4)])
                L.wait(pe, "cols_full", 16)
                L.chunk("kpe", cols[:, C2_KPE:C2_KPE + KC * 64].rearrange("p (k n) -> p k n", k=KC), 0, hx, KC, T2, m=64)
                feature_tile(1, [f"rq{c}" for c in range(4)])
                L.wait(pe, "sq_done", 2)
                L.stats("qa", [sq[:, c, :] for c in (0, 1)], T2)
                L.stats("kva", [sq[:, c, :] for c in (2, 3)], T2)

                def swap(name, perm, m, src):
                    b = L.group(name)
                    pe.sem_inc(held["pe"], 1)
                    i = L.mm(b[0:m, 0:T2], perm, src, True, True, last=True)
                    L.inc(i, "pj_full")

                L.wait(pe, "small_done", 3)
                swap("kperm", swap64, 64, kpg[0:64, :])
                feature_tile(2, [f"rk{c}" for c in range(4)])
                w = tile_ready(pe, L, 3).rearrange("p (k n) -> p k n", k=KC)
                for t, (t0, m) in enumerate(ATILES):
                    L.tokens(f"rv{t}", w, 0, hx, KC, t0, m)
                L.owed = True
                feature_tile(4, [f"rg{c}" for c in range(4)])
                w5 = tile_ready(pe, L, 5)
                wq = w5[:, 0:1536].rearrange("p (k n) -> p k n", k=2)
                wkv = w5[:, 1536:3584].rearrange("p (k n) -> p k n", k=2)
                L.wait(pe, "small_done", 7)
                for h in range(MH):
                    L.chunk(f"qn{h}", wq, h * P, lambda k: cq[:, k, :], 2, T2)
                for h in range(MH):
                    L.chunk(f"qr{h}", wq, 512 + h * 64, lambda k: cq[:, k, :], 2, T2, m=64)
                for h in range(MH):
                    L.chunk(f"kn{h}", wkv, h * P, lambda k: cq[:, 2 + k, :], 2, T2)
                for t, (t0, m) in enumerate(ATILES):
                    L.tokens(f"v{t}", wkv, 512, lambda k: cq[:, 2 + k, :], 2, t0, m)
                L.owed = True
                L.evacuated(pe, "rk3")
                for h in range(RH):
                    swap(f"rqp{h}", swap128, P, rq[:, h, :])
                for h in range(RH):
                    swap(f"rkp{h}", swap128, P, rk[:, h, :])
                L.wait(pe, "sq_done", 4)
                for h in range(MH):
                    L.stats(f"qs{h}", [sq[:, h, :], sq[0:64, 4 + h, :]], T2)
                L.wait(pe, "sq_done", 6)
                for h in range(MH):
                    L.stats(f"ks{h}", [hT[:, h, :], hT[0:64, 4, :]], T2)
                for h in range(MH):
                    L.wait(pe, "small_done", 7 + h + 1)
                    swap(f"qp{h}", swap64, 64, qr[0:64, h, :])

                KTILES = ((0, P, 0, 0), (1, P, P, T2), (2, T2 - 2 * P, 2 * P, 2 * T2 - P))

                def ret_scores(h):
                    L.wait(pe, "rot_done", 2 * (h + 1))
                    L.wait(pe, "s_read", h - 1)
                    for t, m, n0, c0 in KTILES:
                        i = L.mm(S[h % 2][0:m, c0:c0 + T2 - n0], rk[:, h, t * P:t * P + m], rq[:, h, n0:T2], True, True,
                                 last=t == 2)
                    L.inc(i, "s_full")

                def sums(u, buf, val, h):
                    L.wait(pe, "o_read", u)
                    for t, m, n0, c0 in KTILES:
                        i = pe.matmul(O[:, n0:T2], val[0:m, t, h * P:(h + 1) * P], buf[0:m, c0:c0 + T2 - n0],
                                      start=t == 0, stop=t == 2)
                    L.inc(i, "o_full")

                for h in range(RH + 1):
                    if h < RH:
                        ret_scores(h)
                    if h:
                        L.wait(pe, "s_read", h)
                        sums(h - 1, pr[:, (h - 1) % 2, :], rv, h - 1)

                def mla_scores(h):
                    L.wait(pe, "rot_done", 2 * RH + 2 * (h + 1))
                    use = RH + 2 * h
                    for part_, regions in enumerate((((0, P, 0, P), (P, P, P, 2 * P)), ((2 * P, T2 - 2 * P, 0, T2),))):
                        L.wait(pe, "s_read", use + part_ - 1)
                        for q0, m, c0, n in regions:
                            o = S[(use + part_) % 2][0:m, c0:c0 + n]
                            pe.matmul(o, qn[:, h, q0:q0 + m], kn[:, h, 0:n], start=True, stop=False)
                            i = pe.matmul(o, qr[0:64, h, q0:q0 + m], kr[0:64, h, 0:n], start=False, stop=True)
                        L.inc(i, "s_full")

                def mla_turn(h):
                    L.wait(pe, "p_done", h + 1)
                    L.wait(pe, "pt_read", h)
                    p = pr[:, h % 2, :]
                    pe.transpose(PT[:, 0:P], p[:, 0:P], ident)
                    pe.transpose(PT[:, P:2 * P], p[:, P:2 * P], ident)
                    pe.transpose(PT[:, T2:T2 + P], p[:, 2 * P:3 * P], ident)
                    pe.transpose(PT[:, 2 * P:T2], p[0:16, 384:384 + P], ident[0:16, 0:16])
                    pe.transpose(PT[:, T2 + P:T2 + P + 16], p[0:16, 384 + P:384 + 2 * P], ident[0:16, 0:16])
                    i = pe.transpose(PT[0:16, 2 * T2 - P:2 * T2 - P + 16], p[0:16, 384 + 2 * P:384 + T2], ident[0:16, 0:16])
                    L.inc(i, "t_done")

                for h in range(MH + 1):
                    if h < MH:
                        mla_scores(h)
                    if h:
                        mla_turn(h - 1)
                        L.wait(pe, "pt_read", h)
                        sums(RH + h - 1, pt[:, (h - 1) % 2, :], v2, h - 1)

                L.wait(pe, "o_read", RH)
                for h in range(RH):
                    b = L.group(f"rc{h}")
                    L.inc(L.mm(b[:, 0:T2], center, ro[:, h, :], True, True, last=True), "pj_full")
                for h in range(RH):
                    L.wait(pe, "sq_done", 6 + h + 1)
                    L.stats(f"rs{h}", [sq[:, h, :]], T2)
                for h in range(MH):
                    L.wait(pe, "sq_done", 10 + h + 1)
                    L.stats(f"ms{h}", [sq[:, 4 + h, :]], T2)
                L.wait(pe, "y_done", 8)
                for t in range(2):
                    w = tile_ready(pe, L, 6 + t).rearrange("p (k n) -> p k n", k=KC)
                    for c in range(4):
                        L.chunk(f"out{4 * t + c}", w, c * P, lambda k: yT[:, k, :], KC, T2)
                    L.owed = True
                L.wait(pe, "sq_done", 15)
                L.stats("norm2", [sq[:, c, :] for c in range(KC)], T2)
                L.wait(pe, "h_done", 2 * KC)
                for j in range(11):
                    feature_tile(8 + j, [f"g{2 * j}", f"g{2 * j + 1}", f"u{2 * j}", f"u{2 * j + 1}"])
                L.wait(pe, "b2_act", FC)
                for c in range(8):
                    w = tile_ready(pe, L, 19 + c)[:, 0:FC * P].rearrange("p (k n) -> p k n", k=FC)
                    L.chunk(f"dn{c}", w, 0, lambda k: actT[:, k, :], FC, T2)
                    L.owed = True
                L.owed = False
                L.wait(pe, "pj_full", L.n["pj_full"])
                pe.sem_inc(N["w_free"], 1)
                L.n["w_free"] += 1
                L.pad()
                L.check(["pj_full", "w_free", "s_full", "t_done", "o_full", "v_free", "f_full"])

            with pe.Fori(0, DEPTH) as l:
                block1(l)
            L = Products("f", 0)
            L.wait(pe, "sq_done", 1)
            L.stats("normf", [sq[:, c, TX] for c in range(KC)], SEQ)
            L.pad()
            with pe.Fori(0, DEPTH) as l:
                block2(l)

        @block.scalar
        def _(act):
            act.sem_inc(N["evac"], BANKS)
            act.sem_inc(N["pt_read"], 1)
            act.sem_inc(N["o_read"], 1)
            act.wait_ge(memset_done, 1)
            act.wait_ge(setup_pe, 1)
            act.activation(gvec, PJ[0][0:DH, 0:384], ACT.Copy).then_inc(setup_act, 1)
            act.wait_ge(setup_act, 1)
            act.dma_start(scratch[:], gvec).then_inc(scratch_out, 16)
            act.wait_ge(scratch_out, 16)
            act.dma_start(doT[:, 0:DH, :], bass.AP(tensor=scratch, offset=0, ap=[[1, P], [384, DH], [1, 256]]))\
               .then_inc(scratch_in, 16)

            class Copies(Layer):
                def src(self, name):
                    assert PLAN[self.block][self.g] == name, (PLAN[self.block][self.g], name)
                    self.wait(act, "pj_full", self.g + 1)
                    b = PJ[self.g % BANKS]
                    self.g += 1
                    return b

                def out(self, name, dst, n, m0=0, m=P, scale=1.0):
                    b = self.src(name)[m0:m0 + m, 0:n]
                    if len(dst.shape) == 3:
                        b = b.rearrange("p (a n) -> p a n", a=dst.shape[1])
                    self.inc(act.activation(dst, b, ACT.Copy, scale=scale), "evac")

                def mean(self, name, dst, n, width):
                    b = self.src(name)
                    if width == D:
                        act.activation(rstd[:, 7, 0:n], b[:, 0:n], ACT.Identity, scale=1.0 / width, bias=eps[:, 0:1])
                    self.inc(act.activation(dst, b[:, 0:n], ACT.Sqrt, scale=1.0 / width, bias=eps[:, 0:1]), "evac")

                def square(self, dst, src):
                    self.inc(act.activation(dst, src, ACT.Square), "sq_done")

                def pad(self):
                    n = TURNS[self.block] - len(PLAN[self.block])
                    assert self.g == len(PLAN[self.block])
                    if n:
                        self.wait(act, "evac", self.n["evac"])
                        act.sem_inc(N["evac"], n)
                        self.n["evac"] += n

            def block1(l):
                L = Copies(1, l)
                L.wait(act, "x_done", 0)
                L.square(sq[:, :, TX], xT[:, :, TX])
                L.mean("norm1", ms[:, 0, 0:SEQ], SEQ, D)
                for c in range(4):
                    L.out(f"dq{c}", dqT[:, c, :], SEQ, scale=0.125)
                for c in range(4):
                    L.out(f"dk{c}", dkT[:, c, :], SEQ)
                for c in range(2):
                    L.out(f"dv{c}", dv[:, c, :], 512)
                for c in range(4):
                    L.out(f"fq{c}", fqT[:, c, :], SEQ, scale=0.125)
                for c in range(4):
                    L.out(f"fk{c}", fkT[:, c, :], SEQ)
                for c in range(2):
                    L.out(f"fv{c}", fv[:, c, :], 512)
                L.wait(act, "cols_full", 16)
                b = L.src("ff")
                L.inc(act.activation(fox[:, 0, :], b[0:FH, 0:SEQ], ACT.Identity, bias=cols[0:FH, C1_BF:C1_BF + 1]), "evac")
                L.wait(act, "l_done", 1)
                L.inc(act.activation(lam[:, 2:4], lam[:, 0:2], ACT.Exp), "act_misc")
                L.wait(act, "z_done", 1)
                L.inc(act.activation(fox[:, 3, :], fox[:, 2, :], ACT.Exp, scale=-1.0), "act_misc")
                L.wait(act, "act_misc", 2)
                L.inc(act.activation(fox[:, 4, :], fox[:, 3, :], ACT.Ln, bias=eps[0:FH, 1:2]), "act_misc")

                def exps(i):
                    L.wait(act, "s_read", i + 1)
                    if i >= 2:
                        L.wait(act, "p_done", i - 1)
                    for r, (c0, n) in enumerate(((0, P), (P, 2 * P))):
                        L.inc(act.activation(ex[:, i % 2, c0:c0 + n], nl[:, i % 2, c0:c0 + n], ACT.Exp, scale=-1.0,
                                             bias=nmax[:, i % 2, r:r + 1], accum_out=esum[:, i % 2, r:r + 1]), "e_done")

                def turned(u):
                    L.wait(act, "t_done", u + 1)
                    if u >= 2:
                        L.wait(act, "o_full", u - 1)
                    L.inc(act.activation(pt[:, u % 2, 0:384], PT[:, 0:384], ACT.Copy), "pt_read")

                def outputs(u):
                    L.wait(act, "o_full", u + 1)
                    if u < DH:
                        i = act.activation(ydT[:, u, :], O[:, 0:SEQ], ACT.Copy)
                    else:
                        r = slice(64 * (u % 2), 64 * (u % 2) + 64)
                        i = act.activation(yfT[r, (u - DH) // 2, :], O[r, 0:SEQ], ACT.Copy)
                    L.inc(i, "o_read")

                for i in range(MAPS + 2):
                    if i < MAPS:
                        exps(i)
                        b = L.src(f"gate{i}")
                        L.inc(act.activation(gate[:, i, :], b[:, 0:SEQ], ACT.Tanh, scale=0.5), "evac")
                    if i - 1 in UNIT:
                        turned(UNIT[i - 1])
                    if i - 2 in UNIT:
                        outputs(UNIT[i - 2])
                L.wait(act, "o_read", DH + FH)
                L.square(sq[:, 0:DH, TX], ydT)
                for h in range(DH):
                    L.mean(f"dnorm{h}", ms[:, h, 0:SEQ], SEQ, P)
                for c in range(8):
                    L.out(f"do{c}", doT[:, c, :], SEQ, scale=0.5)
                for c in range(8):
                    L.out(f"fo{c}", foT[:, c, :], SEQ, scale=0.5)
                for c in range(8):
                    L.out(f"out{c}", oTmp[:, c, :], SEQ)
                L.wait(act, "x_done", KC)
                L.square(sq[:, :, TX], xT[:, :, TX])
                L.mean("norm2", ms[:, 0, 0:SEQ], SEQ, D)
                for c in range(4):
                    L.out(f"hn{c}", h2n[:, c // 2, (c % 2) * 512:(c % 2 + 1) * 512], 512)
                for c in range(16):
                    L.out(f"wq{c}", qT[:, c, :], SEQ)
                for c in range(8):
                    L.out(f"s{c}", (sc, sc1)[c // 4][:, 4 * (c % 4):4 * (c % 4) + 4, :], 512)
                for tt in range(2):
                    L.wait(act, "gmax", tt + 1)
                    L.inc(act.activation(gates[:], gates[:], ACT.Exp), "act_misc")
                    with act.Fori(0, SLOTS // (8 * GB)) as j:
                        for g in range(8):
                            act.wait_ge(N["u_free"], L.at("u_free", tt * SLOTS + GB * (g + 1)) + j * (8 * GB))
                            act.activation(gl[:, g % 2, :], dots[:, g % 2, :], ACT.Gelu).then_inc(N["gelu_done"], 1)
                    L.n["gelu_done"] = L.n.get("gelu_done", 0) + SLOTS // GB
                    L.wait(act, "f_full", tt + 1)
                    for n in range(2):
                        L.inc(act.activation(fn[:, n * 512:(n + 1) * 512], S[n][:], ACT.Copy), "f_read")
                    for hf in range(2):
                        L.out(f"ft{2 * tt + hf}", fT[:, 4 * hf:4 * hf + 4, :], 512)
                L.pad()
                L.check(["evac", "sq_done", "e_done", "pt_read", "o_read", "act_misc", "gelu_done", "f_read"])

            def block2(l):
                L = Copies(2, l)
                L.wait(act, "x_done", 0)
                L.square(sq[:], xT[:])
                L.mean("norm1", ms[:, 0, :], T2, D)
                for c in range(4):
                    L.out(f"cq{c}", cq[:, c, :], T2)
                L.evacuated(act, "cq3")
                L.square(sq[:, 0:4, :], cq)
                L.out("kpe", kpe[0:64, :], T2, m=64)
                for c in range(4):
                    L.out(f"rq{c}", rq[:, c, :], T2)
                L.mean("qa", ms[:, 0, :], T2, 256)
                L.mean("kva", ms[:, 1, :], T2, 256)
                L.out("kperm", tmpP[0:64, 4, :], T2, m=64)
                for c in range(4):
                    L.out(f"rk{c}", rk[:, c, :], T2)
                for t, (t0, m) in enumerate(ATILES):
                    L.out(f"rv{t}", rv[0:m, t, :], 512, m=m)
                for c in range(4):
                    b = L.src(f"rg{c}")
                    act.activation(rgt[:, c, :], b[:, 0:T2], ACT.Tanh, scale=0.5)
                    L.inc(act.activation(rgr[:, c, :], b[:, 0:T2], ACT.Copy, scale=0.5), "evac")
                for h in range(MH):
                    L.out(f"qn{h}", qn[:, h, :], T2)
                for h in range(MH):
                    L.out(f"qr{h}", qr[0:64, h, :], T2, m=64)
                for h in range(MH):
                    L.out(f"kn{h}", kn[:, h, :], T2)
                for t, (t0, m) in enumerate(ATILES):
                    L.out(f"v{t}", v2[0:m, t, :], 512, m=m)
                L.evacuated(act, "kn3")
                L.square(sq[:, 0:4, :], qn)
                L.square(sq[0:64, 4:8, :], qr[0:64, :, :])
                L.square(hT[:, 0:4, :], kn)
                L.square(hT[0:64, 4, :], kpe[0:64, :])
                for h in range(RH):
                    L.out(f"rqp{h}", tmpR[:, h, :], T2)
                for h in range(RH):
                    L.out(f"rkp{h}", tmpR[:, 4 + h, :], T2)
                for h in range(MH):
                    L.mean(f"qs{h}", ms[:, h, :], T2, QKH)
                for h in range(MH):
                    L.wait(act, "rstd", 3 + h + 1)
                    L.mean(f"ks{h}", ms[:, h, :], T2, QKH)
                for h in range(MH):
                    L.out(f"qp{h}", tmpP[0:64, h, :], T2, m=64)

                def outputs(u):
                    L.wait(act, "o_full", u + 1)
                    L.inc(act.activation((ro if u < RH else mo)[:, u % 4, :], O[:, 0:T2], ACT.Copy), "o_read")

                for h in range(RH):
                    outputs(h)
                for h in range(MH + 1):
                    if h < MH:
                        for r, (m, c0, n) in enumerate(((P, 0, P), (P, P, 2 * P), (16, 384, T2))):
                            if r == 0:
                                L.wait(act, "s_read", RH + 2 * h + 1)
                                if h >= 2:
                                    L.wait(act, "p_done", h - 1)
                            if r == 2:
                                L.wait(act, "s_read", RH + 2 * h + 2)
                            L.inc(act.activation(ex[0:m, h % 2, c0:c0 + n], nl[0:m, h % 2, c0:c0 + n], ACT.Exp,
                                                 scale=-1.0, bias=nmax[0:m, h % 2, r:r + 1],
                                                 accum_out=esum[0:m, h % 2, r:r + 1]), "e_done")
                    if h:
                        L.wait(act, "t_done", h)
                        if h >= 3:
                            L.wait(act, "o_full", RH + h - 2)
                        act.activation(pt[:, (h - 1) % 2, 0:416], PT[:, 0:416], ACT.Copy)
                        L.inc(act.activation(pt[0:16, (h - 1) % 2, 416:432], PT[0:16, 416:432], ACT.Copy), "pt_read")
                        outputs(RH + h - 1)
                for h in range(RH):
                    L.out(f"rc{h}", ro[:, h, :], T2)
                for h in range(RH):
                    L.evacuated(act, f"rc{h}")
                    L.square(sq[:, h, :], ro[:, h, :])
                L.wait(act, "o_read", RH + MH)
                for h in range(MH):
                    L.square(sq[:, 4 + h, :], mo[:, h, :])
                L.wait(act, "rstd", 3 + 2 * MH)
                for h in range(RH):
                    L.mean(f"rs{h}", ms[:, h, :], T2, P)
                for h in range(MH):
                    L.wait(act, "rstd", 3 + 2 * MH + h + 1)
                    L.mean(f"ms{h}", ms[:, h, :], T2, P)
                for c in range(8):
                    L.out(f"out{c}", oTmp2[:, c, :], T2)
                L.wait(act, "x_done", KC)
                L.square(sq[:], xT[:])
                L.mean("norm2", ms[:, 0, :], T2, D)
                for j in range(11):
                    if j >= 2:
                        L.wait(act, "b2_act", 2 * (j - 1))
                    for i in range(2):
                        b = L.src(f"g{2 * j + i}")
                        act.activation(gbuf[:, j % 2, i, :], b[:, 0:T2], ACT.Tanh, scale=0.5)
                        L.inc(act.activation(gbuf[:, j % 2, 2 + i, :], b[:, 0:T2], ACT.Copy, scale=0.5), "evac")
                    for i in range(2):
                        L.out(f"u{2 * j + i}", gbuf[:, j % 2, 4 + i, :], T2)
                for c in range(8):
                    L.out(f"dn{c}", oTmp2[:, c, :], T2)
                L.pad()
                L.check(["evac", "sq_done", "e_done", "pt_read", "o_read", "act_misc", "gelu_done", "f_read"])

            with act.Fori(0, DEPTH) as l:
                block1(l)
            L = Copies("f", 0)
            L.wait(act, "x_done", 0)
            L.square(sq[:, :, TX], xT[:, :, TX])
            L.mean("normf", ms[:, 0, 0:SEQ], SEQ, D)
            L.pad()
            with act.Fori(0, DEPTH) as l:
                block2(l)

        @block.vector
        def _(dve):
            tt_ = dve.tensor_tensor
            stt = dve.scalar_tensor_tensor
            dve.memset(ones[:], 1.0)
            dve.memset(loff[:], 0.0)
            dve.memset(eps[:, 2:3], -0.5)
            dve.memset(eps[:, 3:4], 0.0)
            dve.memset(idxf[:], 0.0)
            dve.memset(eps[:, 0:1], EPS)
            dve.memset(eps[:, 1:2], 1.0).then_inc(memset_done, 1)
            dve.wait_ge(const_full, 96)
            dve.wait_ge(memset_done, 1)
            dve.tensor_scalar(nsel[:], kst[0:FH, K_ID:K_ID + FH], -1.0, None, ALU.mult)
            dve.wait_ge(setup_pe, 2)
            for h in range(DH):
                tt_(bias[:, h, 0:P], PJ[h][:, P:2 * P], mask[:, 0:P], ALU.add)
                tt_(bias[:, h, P:2 * P], PJ[h][:, 0:P], mask[:, P:2 * P], ALU.add)
                m = tt_(bias[:, h, 2 * P:3 * P], PJ[h][:, P:2 * P], mask[:, 2 * P:3 * P], ALU.add)
            m.then_inc(setup_dve, 1)
            dve.wait_ge(setup_dve, 1)
            dve.sem_inc(N["s_read"], 2)
            dve.sem_inc(N["u_free"], UB)
            dve.sem_inc(N["diag_done"], 1)
            dve.sem_inc(N["x_done"], 1)

            class Steps(Layer):
                def step(self, ins):
                    self.inc(ins, "dve_misc")

                def settle(self, held_=False):
                    k = self.n["dve_misc"]
                    (self.hold(dve, "dve", "dve_misc", k) if held_ else self.wait(dve, "dve_misc", k))

                def root(self, group, i, o, n):
                    self.evacuated(dve, group)
                    if not group.startswith("norm"):
                        self.inc(dve.reciprocal(rstd[:, o, 0:n], ms[:, i, 0:n]), "rstd")
                        self.wait(dve, "rstd", self.n["rstd"])
                        return
                    r, t, m = rstd[:, o, 0:n], ms[:, i, 0:n], rstd[:, 7, 0:n]
                    self.step(dve.reciprocal(r, t))
                    self.settle()
                    self.step(stt(t, m, -0.5, r, ALU.mult, ALU.mult))
                    self.settle()
                    self.step(tt_(t, t, r, ALU.mult))
                    self.settle()
                    self.inc(stt(r, t, 1.5, r, ALU.add, ALU.mult), "rstd")
                    self.wait(dve, "rstd", self.n["rstd"])

                def norm(self, dst, src, gain, r, name):
                    for c in range(len(dst)):
                        self.inc(stt(dst[c], src[c], gain[c], r, ALU.mult, ALU.mult), name)

            def block1(l):
                L = Steps(1, l)
                L.wait(dve, "cols_full", 16)
                for a in range(2):
                    o = C1_LAM + 128 * a
                    m = dve.tensor_tensor_reduce(out=junk[:] if a else zjunk[:], in0=cols[:, o:o + 64],
                                                 in1=cols[:, o + 64:o + 128],
                                                 scale=1.0, scalar=0.0, op0=ALU.mult, op1=ALU.add,
                                                 accum_out=lam[:, a:a + 1])
                L.inc(m, "l_done")
                L.root("norm1", 0, 0, SEQ)
                L.norm([hT[:, c, TX] for c in range(KC)], [xT[:, c, TX] for c in range(KC)],
                       [cols[:, C1_N1 + c:C1_N1 + c + 1] for c in range(KC)], rstd[:, 0, 0:SEQ], "h_done")
                L.evacuated(dve, "ff")
                L.step(dve.tensor_scalar(fox[:, 1, :], fox[:, 0, :], 0.0, None, ALU.min))
                L.settle()
                L.inc(stt(fox[:, 2, :], fox[:, 1, :], -2.0, fox[:, 0, :], ALU.mult, ALU.add), "z_done")
                L.wait(dve, "act_misc", 1)
                L.step(tt_(lam[:, 4:5], lam[:, 3:4], lam[:, 2:3], ALU.subtract))
                L.settle()
                tt_(lam[:, 5:6], lam[:, 4:5], cols[:, C1_LI:C1_LI + 1], ALU.subtract)
                L.step(tt_(lam[:, 6:7], cols[:, C1_SUB:C1_SUB + 1], cols[:, C1_LI + 1:C1_LI + 2], ALU.mult))
                L.wait(dve, "act_misc", 3)
                L.step(tt_(fox[:, 4, :], fox[:, 1, :], fox[:, 4, :], ALU.subtract))
                L.settle()
                L.inc(dve.tensor_tensor_scan(fox[:, 5, :], eps[0:FH, 1:2].to_broadcast([FH, SEQ]), fox[:, 4, :], 0.0,
                                             ALU.mult, ALU.add), "c_done")

                def logits(i):
                    L.wait(dve, "s_full", i + 1)
                    dve.sem_inc(held["dve"], 1)
                    if i >= 2:
                        L.hold(dve, "dve", "e_done", 2 * (i - 1))
                    b = bias[:, i // 2, :] if i < 2 * DH else mask
                    for r, (c0, n) in enumerate(((0, P), (P, 2 * P))):
                        m = dve.tensor_tensor_reduce(out=nl[:, i % 2, c0:c0 + n], in0=S[i % 2][:, c0:c0 + n],
                                                     in1=b[:, c0:c0 + n], scale=-1.0, scalar=BIG, op0=ALU.add,
                                                     op1=ALU.min, accum_out=nmax[:, i % 2, r:r + 1])
                    L.inc(m, "s_read")

                def probs(i):
                    p, u = i % 2, UNIT.get(i, i // 2)
                    L.wait(dve, "e_done", 2 * (i + 1))
                    L.step(dve.reciprocal(erec[:, p, 0:2], esum[:, p, 0:2]))
                    L.settle()
                    if i < 2 * DH and i % 2:
                        L.step(dve.tensor_scalar(erec[:, p, 0:2], erec[:, p, 0:2], lam[:, 5:6], None, ALU.mult))
                        L.settle()
                        for r, (c0, n) in enumerate(((0, P), (P, 2 * P))):
                            m = stt(pr[:, u % 2, c0:c0 + n], ex[:, p, c0:c0 + n], erec[:, p, r:r + 1],
                                    pr[:, u % 2, c0:c0 + n], ALU.mult, ALU.add)
                    else:
                        if u >= 2:
                            L.wait(dve, "t_done", u - 1)
                        for r, (c0, n) in enumerate(((0, P), (P, 2 * P))):
                            m = dve.tensor_scalar(pr[:, u % 2, c0:c0 + n], ex[:, p, c0:c0 + n], erec[:, p, r:r + 1],
                                                  None, ALU.mult)
                    L.inc(m, "p_done")

                for i in range(MAPS + 1):
                    if i < MAPS:
                        logits(i)
                    if i:
                        probs(i - 1)

                L.wait(dve, "h_done", KC)
                for h in range(DH):
                    L.root(f"dnorm{h}", h, h, SEQ)
                    L.inc(stt(ydT[:, h, :], ydT[:, h, :], lam[:, 6:7], rstd[:, h, 0:SEQ], ALU.mult, ALU.mult), "y_done")
                for c in range(8):
                    L.evacuated(dve, f"fo{c}")
                    stt(doT[:, c, :], gate[:, c, :], 1.0, doT[:, c, :], ALU.add, ALU.mult)
                    L.step(stt(foT[:, c, :], gate[:, 8 + c, :], 1.0, foT[:, c, :], ALU.add, ALU.mult))
                    L.settle()
                    L.inc(tt_(mgT[:, c, :], doT[:, c, :], foT[:, c, :], ALU.add), "y_done")
                for c in range(8):
                    L.evacuated(dve, f"out{c}")
                    L.inc(tt_(xT[:, c, TX], xT[:, c, TX], oTmp[:, c, :], ALU.add), "x_done")
                L.wait(dve, "y_done", DH)
                L.root("norm2", 0, 0, SEQ)
                L.norm([hT[:, c, TX] for c in range(KC)], [xT[:, c, TX] for c in range(KC)],
                       [cols[:, C1_N2 + c:C1_N2 + c + 1] for c in range(KC)], rstd[:, 0, 0:SEQ], "h_done")

                def route(tt):
                    s = (sc, sc1)[tt]

                    def top16(src, vals, poss):
                        for a in range(2):
                            for v, x in zip(vals, src):
                                m = dve.max(v[:, 8 * a:8 * a + 8], x)
                            L.step(m)
                            L.settle(True)
                            for v, x, q in zip(vals, src, poss):
                                m = dve.max_index(q[:, 8 * a:8 * a + 8], v[:, 8 * a:8 * a + 8], x)
                            L.step(m)
                            if a == 0:
                                L.settle(True)
                                for v, x in zip(vals, src):
                                    m = dve.match_replace(x, v[:, 0:8], x, -3e38)
                                L.step(m)
                                L.settle(True)

                    L.hold(dve, "dve", "evac", GI[1][f"s{4 * tt + 3}"] + 1)
                    top16([s[:, i, :] for i in range(16)], [topv[:, i, :] for i in range(16)],
                          [topi[:, i, :] for i in range(16)])
                    L.settle()
                    t4 = lambda x: x.rearrange("p (h a) k -> p h a k", a=2)
                    dve.tensor_scalar(t4(topf)[:, :, 0, :], t4(topi)[:, :, 0, :], 128.0, loff[:, 0:1], ALU.mult, ALU.add)
                    L.step(dve.tensor_copy(t4(topf)[:, :, 1, :], t4(topi)[:, :, 1, :]))
                    L.settle()
                    for dst, src in ((cnd, topv), (cidx, topf)):
                        off = 0
                        for i0, ni, nj in RANKS:
                            m = tt_(dst[:, :, off:off + ni * nj].rearrange("p h (a b) -> p h a b", a=ni),
                                    t4(src)[:, :, 0, i0:i0 + ni].unsqueeze(3).to_broadcast([P, PH, ni, nj]),
                                    t4(src)[:, :, 1, 0:nj].unsqueeze(2).to_broadcast([P, PH, ni, nj]), ALU.add)
                            off += ni * nj
                    L.step(m)
                    L.settle(True)
                    top16([cnd[:, h, :] for h in range(PH)], [bestv[:, h, :] for h in range(PH)],
                          [bestp[:, h, :] for h in range(PH)])
                    L.settle()
                    L.step(dve.tensor_copy(bestf, bestp))
                    L.settle()
                    for c in range(PH // 2):
                        L.step(tt_(eq, iota.unsqueeze(1).to_broadcast([P, 32, CAND]),
                                   bestf[:, 2 * c:2 * c + 2, :].rearrange("p h k -> p (h k)").unsqueeze(2)
                                   .to_broadcast([P, 32, CAND]), ALU.is_equal))
                        L.settle()
                        e4 = eq.rearrange("p (h k) c -> p h k c", h=2)
                        L.step(tt_(e4, e4, cidx[:, 2 * c:2 * c + 2, :].unsqueeze(2).to_broadcast([P, 2, TOPK, CAND]), ALU.mult))
                        L.settle()
                        L.step(dve.tensor_reduce(idxf[:, 32 * c:32 * c + 32], eq, AX.X, ALU.add))
                        L.settle()
                        if c == 0:
                            if tt:
                                L.wait(dve, "v_free", tt * SLOTS)
                            L.inc(dve.tensor_copy(idx[:, 0:TOPK], idxf[:, 0:TOPK]), "idx_a")
                    L.inc(tt_(gates[:], bestv, bestv[:, :, 0:1].to_broadcast([P, PH, TOPK]), ALU.subtract), "gmax")
                    L.wait(dve, "act_misc", 3 + tt + 1)
                    L.step(dve.tensor_reduce(gsum[:, 0, :], gates[:], AX.X, ALU.add))
                    L.settle()
                    L.step(dve.reciprocal(gsum[:, 1, :], gsum[:, 0, :]))
                    L.settle()
                    L.step(tt_(gates[:], gates[:], gsum[:, 1, :].unsqueeze(2).to_broadcast([P, PH, TOPK]), ALU.mult))

                gflat = gates[:].rearrange("p h k -> p (h k)")

                def experts(tt):
                    base = L.n["dve_misc"]
                    L.settle(True)
                    with dve.Fori(0, SLOTS // (8 * GB)) as j:
                        for g in range(8):
                            for i in range(GB):
                                b = GB * (g % 2) + i
                                dve.wait_ge(u_full[b], L.l * (32 * SLOTS // UB) + j * 64
                                            + 16 * (tt * SLOTS // UB + g // 2 + 1))
                                dve.tensor_tensor_reduce(out=urow[:, b, :], in0=urow[:, b, :], in1=h2n[:, tt, :],
                                                         scale=1.0, scalar=0.0, op0=ALU.mult, op1=ALU.add,
                                                         accum_out=dots[:, g % 2, i:i + 1]).then_inc(N["u_free"], 1)
                            if g == 1:
                                dve.wait_ge(N["v_free"], L.at("v_free", tt * SLOTS) + j * (8 * GB))
                                dve.tensor_scalar(idx[:, TOPK:2 * TOPK], idxf[:, bass.ds(j * 32 + 16, TOPK)], 0.0, None,
                                                  ALU.add).then_inc(N["idx_b"], 1)
                            if g == 5:
                                dve.wait_ge(N["v_free"], L.at("v_free", tt * SLOTS + 4 * GB) + j * (8 * GB))
                                dve.tensor_scalar(idx[:, 0:TOPK], idxf[:, bass.ds(j * 32 + 32, TOPK)], 0.0, None,
                                                  ALU.add).then_inc(N["idx_a"], 1)
                            dve.wait_ge(N["gelu_done"], L.at("gelu_done", tt * SLOTS // GB + g + 1) + j * 8)
                            dve.wait_ge(N["diag_done"], L.at("diag_done", tt * SLOTS + GB * g) + j * (8 * GB))
                            tt_(wgt[:, g % 2, :], gl[:, g % 2, :], gflat[:, bass.ds(j * 32 + GB * g, GB)], ALU.mult)\
                                .then_inc(N["dve_misc"], 1)
                            dve.wait_ge(N["dve_misc"], L.at("dve_misc", base + g + 1) + j * 8)
                            dve.wait_ge(N["v_free"], L.at("v_free", tt * SLOTS + GB * (g - 1)) + j * (8 * GB))
                            for i in range(GB):
                                b = GB * (g % 2) + i
                                dve.tensor_scalar(diag[:, b, :], ident, wgt[:, g % 2, i:i + 1], None, ALU.mult)\
                                   .then_inc(N["diag_done"], 1)
                    for n, k in (("u_free", SLOTS), ("idx_a", SLOTS // 32), ("idx_b", SLOTS // 32),
                                 ("diag_done", SLOTS), ("dve_misc", SLOTS // GB)):
                        L.n[n] = L.n.get(n, 0) + k

                def add(tt):
                    for hf in range(2):
                        L.evacuated(dve, f"ft{2 * tt + hf}")
                        x = xT[:, 4 * hf:4 * hf + 4, META + tt * P:META + (tt + 1) * P]
                        L.inc(tt_(x, x, fT[:, 4 * hf:4 * hf + 4, :], ALU.add), "x_done")

                route(0)
                L.step(dve.tensor_copy(junk[:, 0:1], loff[:]))
                experts(0)
                route(1)
                add(0)
                experts(1)
                add(1)
                L.step(dve.tensor_scalar(loff[:], loff[:], float(NEXP), None, ALU.add))
                L.check(["rstd", "h_done", "s_read", "p_done", "x_done", "y_done", "c_done", "z_done", "l_done", "gmax", "idx_a",
                         "idx_b", "u_free", "diag_done", "dve_misc"])

            def block2(l):
                L = Steps(2, l)
                col = lambda c, m=P: cols[0:m, c:c + 1]
                L.wait(dve, "cols_full", 16)
                L.inc(dve.tensor_scalar(lam[:, 0:2], cols[:, C2_QG:C2_QG + 2], QKH ** -0.5, None, ALU.mult), "small_done")
                L.root("norm1", 0, 0, T2)
                L.norm([hT[:, c, :] for c in range(KC)], [xT[:, c, :] for c in range(KC)],
                       [col(C2_N1 + c) for c in range(KC)], rstd[:, 0, :], "h_done")
                L.evacuated(dve, "kpe")
                L.inc(dve.tensor_scalar(kpg[0:64, :], kpe[0:64, :], col(C2_KG + 1, 64), None, ALU.mult), "small_done")
                dve.wait_ge(const2_full, 16)
                L.wait(dve, "small_done", 2)
                L.inc(tt_(kro[0:64, :], kpg[0:64, :], cosM, ALU.mult), "small_done")
                L.root("qa", 0, 1, T2)
                L.root("kva", 1, 2, T2)
                L.norm([cq[:, c, :] for c in (0, 1)], [cq[:, c, :] for c in (0, 1)], [col(C2_QA + c) for c in range(2)],
                       rstd[:, 1, :], "small_done")
                L.norm([cq[:, c, :] for c in (2, 3)], [cq[:, c, :] for c in (2, 3)], [col(C2_KVA + c) for c in range(2)],
                       rstd[:, 2, :], "small_done")
                L.evacuated(dve, "kperm")
                L.step(tt_(tmpP[0:64, 4, :], tmpP[0:64, 4, :], sinM, ALU.mult))
                L.settle()
                L.step(tt_(kro[0:64, :], kro[0:64, :], tmpP[0:64, 4, :], ALU.add))

                def rotate(x, t, c, s):
                    tt_(t, t, s, ALU.mult)
                    L.step(tt_(x, x, c, ALU.mult))
                    L.settle()
                    return tt_(x, x, t, ALU.add)

                L.wait(dve, "small_done", 7)
                for h in range(MH):
                    L.root(f"qs{h}", h, h, T2)
                    L.step(stt(qn[:, h, :], qn[:, h, :], lam[:, 0:1], rstd[:, h, :], ALU.mult, ALU.mult))
                    L.inc(stt(qr[0:64, h, :], qr[0:64, h, :], lam[0:64, 1:2], rstd[0:64, h, :], ALU.mult, ALU.mult), "small_done")
                for h in range(RH):
                    L.evacuated(dve, f"rkp{h}")
                    for x, t in ((rq, h), (rk, 4 + h)):
                        L.inc(rotate(x[:, h, :], tmpR[:, t, :], cosR, sinR), "rot_done")
                for h in range(RH):
                    L.wait(dve, "s_full", h + 1)
                    if h >= 2:
                        L.wait(dve, "o_full", h - 1)
                    dh = k2st[:, K2_D + 432 * h:K2_D + 432 * (h + 1)]
                    tt_(pr[:, h % 2, 0:416], S[h % 2][:, 0:416], dh[:, 0:416], ALU.mult)
                    L.inc(tt_(pr[0:16, h % 2, 416:432], S[h % 2][0:16, 416:432], dh[0:16, 416:432], ALU.mult), "s_read")
                for h in range(MH):
                    L.root(f"ks{h}", h, 4 + h, T2)
                    L.step(stt(kn[:, h, :], kn[:, h, :], col(C2_KG), rstd[:, 4 + h, :], ALU.mult, ALU.mult))
                    L.inc(tt_(kr[0:64, h, :], kro[0:64, :], rstd[0:64, 4 + h, :], ALU.mult), "rot_done")
                    L.evacuated(dve, f"qp{h}")
                    L.inc(rotate(qr[0:64, h, :], tmpP[0:64, h, :], cosM, sinM), "rot_done")

                REG = ((P, 0, P, 0), (P, P, 2 * P, 0), (16, 384, T2, 1))

                def logits(h):
                    use = RH + 2 * h
                    if h == 0:
                        L.wait(dve, "o_full", RH)
                    if h >= 2:
                        L.hold(dve, "dve", "e_done", 3 * (h - 1))
                    for r, (m, c0, n, bk) in enumerate(REG):
                        if r != 1:
                            L.hold(dve, "dve", "s_full", use + bk + 1)
                        s0 = 0 if r == 2 else c0
                        i = dve.tensor_tensor_reduce(out=nl[0:m, h % 2, c0:c0 + n], in0=S[(use + bk) % 2][0:m, s0:s0 + n],
                                                     in1=k2st[0:m, K2_MASK:K2_MASK + n] if r == 2 else mask[:, c0:c0 + n], scale=-1.0, scalar=BIG,
                                                     op0=ALU.add, op1=ALU.min, accum_out=nmax[0:m, h % 2, r:r + 1])
                        if r:
                            L.inc(i, "s_read")

                def probs(h):
                    p = h % 2
                    L.wait(dve, "e_done", 3 * (h + 1))
                    dve.reciprocal(erec[:, p, 0:2], esum[:, p, 0:2])
                    L.step(dve.reciprocal(erec[0:16, p, 2:3], esum[0:16, p, 2:3]))
                    if h >= 2:
                        L.wait(dve, "t_done", h - 1)
                    L.settle()
                    for r, (m, c0, n, bk) in enumerate(REG):
                        i = dve.tensor_scalar(pr[0:m, p, c0:c0 + n], ex[0:m, p, c0:c0 + n], erec[0:m, p, r:r + 1], None,
                                              ALU.mult)
                    L.inc(i, "p_done")

                for h in range(MH + 1):
                    if h < MH:
                        logits(h)
                    if h:
                        probs(h - 1)
                for h in range(RH):
                    L.step(stt(rgr[:, h, :], rgt[:, h, :], 1.0, rgr[:, h, :], ALU.add, ALU.mult))
                for h in range(RH):
                    L.root(f"rs{h}", h, h, T2)
                    L.step(stt(ro[:, h, :], ro[:, h, :], col(C2_RG + h), rstd[:, h, :], ALU.mult, ALU.mult))
                    L.settle()
                    L.inc(stt(yT[:, 4 + h, :], ro[:, h, :], col(C2_RB + h), rgr[:, h, :], ALU.add, ALU.mult), "y_done")
                for h in range(MH):
                    L.root(f"ms{h}", h, 4 + h, T2)
                    L.inc(stt(yT[:, h, :], mo[:, h, :], col(C2_MO + h), rstd[:, 4 + h, :], ALU.mult, ALU.mult), "y_done")
                for c in range(8):
                    L.evacuated(dve, f"out{c}")
                    L.inc(tt_(xT[:, c, :], xT[:, c, :], oTmp2[:, c, :], ALU.add), "x_done")
                L.root("norm2", 0, 0, T2)
                L.norm([hT[:, c, :] for c in range(KC)], [xT[:, c, :] for c in range(KC)],
                       [col(C2_N2 + c) for c in range(KC)], rstd[:, 0, :], "h_done")
                for j in range(11):
                    for i in range(2):
                        g = gbuf[:, j % 2, :, :]
                        L.evacuated(dve, f"u{2 * j + i}")
                        L.step(stt(g[:, i, :], g[:, i, :], 1.0, g[:, 2 + i, :], ALU.add, ALU.mult))
                        L.settle()
                        L.inc(tt_(actT[:, 2 * j + i, :], g[:, i, :], g[:, 4 + i, :], ALU.mult), "b2_act")
                for c in range(8):
                    L.evacuated(dve, f"dn{c}")
                    L.inc(tt_(xT[:, c, :], xT[:, c, :], oTmp2[:, c, :], ALU.add), "x_done")
                L.check(["rstd", "h_done", "s_read", "p_done", "x_done", "y_done", "small_done", "rot_done", "b2_act", "dve_misc"])

            with dve.Fori(0, DEPTH) as l:
                block1(l)
            L = Steps("f", 0)
            L.root("normf", 0, 0, SEQ)
            L.norm([xT[:, c, TX] for c in range(KC)], [xT[:, c, TX] for c in range(KC)],
                   [fing[:, c:c + 1] for c in range(KC)], rstd[:, 0, 0:SEQ], "x_done")
            with dve.Fori(0, DEPTH) as l:
                block2(l)

        @block.gpsimd
        def _(pool):
            pool.wait_ge(memset_done, 1)
            table_u, table_v = (t.rearrange("l e d -> (l e) d") for t in (eu, ev))

            def params(L, src, n):
                L.hold(pool, "pool", "x_done", 0)
                L.inc(pool.dma_start(cols[:, 0:n], src[L.l, :, :]), "cols_full", 16)

            def gather(rows, table, col, b, full):
                pool.indirect_dma_start(out=rows[:, b, :], out_offset=None, in_=table,
                                        in_offset=bass.IndirectOffsetOnAxis(ap=idx[:, col:col + 1], axis=0))\
                    .then_inc(full[b], 16)

            def block1(l):
                L = Layer(1, l)
                params(L, c1_in, NC1)
                for tt in range(2):
                    with pool.Fori(0, SLOTS // (8 * GB)) as j:
                        def rows_u(g):
                            if g == 0:
                                pool.wait_ge(N["idx_a"], L.at("idx_a", tt * (SLOTS // 32 + 1) + 1) + j)
                            if g == 4:
                                pool.wait_ge(N["idx_b"], L.at("idx_b", tt * (SLOTS // 32) + 1) + j)
                                pool.sem_inc(held["pool"], 1)
                            pool.wait_ge(N["u_free"], L.at("u_free", tt * SLOTS + GB * (g - 1)) + j * (8 * GB))
                            pool.sem_inc(held["pool"], 1)
                            for i in range(GB):
                                gather(urow, table_u, GB * g + i, GB * (g % 2) + i, u_full)

                        def rows_v(g):
                            pool.wait_ge(N["v_free"], L.at("v_free", tt * SLOTS + GB * (g - 1)) + j * (8 * GB))
                            pool.sem_inc(held["pool"], 1)
                            for i in range(GB):
                                gather(vrow, table_v, GB * g + i, GB * (g % 2) + i, v_full)

                        rows_u(0)
                        for g in range(8):
                            if g < 7:
                                rows_u(g + 1)
                            rows_v(g)
                L.check(["cols_full"])

            def block2(l):
                L = Layer(2, l)
                params(L, c2_in, NC2)
                L.check(["cols_full"])

            with pool.Fori(0, DEPTH) as l:
                block1(l)
            L = Layer("f", 0)
            L.wait(pool, "x_done", 0)
            pool.dma_start(k2st, k2_in).then_inc(const2_full, 16)
            with pool.Fori(0, DEPTH) as l:
                block2(l)


def chunks(w, n):
    k = w.shape[0] // P
    return w.reshape(k, P, w.shape[1] // n, n).transpose(2, 1, 0, 3).reshape(w.shape[1] // n, P, k * n)


def wide(t):
    out = np.zeros(t.shape[:-1] + (TILE,), t.dtype)
    out[..., :t.shape[-1]] = t
    return out


def column(v, rows=P):
    return v.reshape(-1, rows).T


def layout_stream(a):
    tiles = []
    for l in range(DEPTH):
        w = a["w_in"][l]
        cut = np.cumsum([512, 512, 512, 512, 512, 512, FH])
        dq, dk, dv_, fq, fk, fv_, ff, gates_ = np.split(w, cut, axis=1)
        for x in (dq, dk, dv_, fq, fk, fv_, gates_):
            tiles.append(chunks(x, 512))
        tiles.append(chunks(a["w_diff_o"][l], 1024))
        tiles.append(chunks(a["w_fox_o"][l], 1024))
        tiles.append(chunks(a["w_out"][l], 512))
        tiles.append(chunks(a["w_query"][l], 512))
    for l in range(DEPTH):
        w = a["w_in_2"][l]
        tiles.append(chunks(w[:, 0:512], 512))
        tiles.append(chunks(w[:, 576:2624], 512))
        q = a["w_q_b_2"][l].reshape(256, MH, QKH)
        q = np.concatenate([q[:, :, :P].reshape(256, -1), q[:, :, P:].reshape(256, -1)], axis=1)
        kv = a["w_kv_b_2"][l].reshape(256, MH, 2 * P)
        kv = np.concatenate([kv[:, :, :P].reshape(256, -1), kv[:, :, P:].reshape(256, -1)], axis=1)
        tiles.append(wide(np.concatenate([chunks(q, 768), chunks(kv, 1024)], axis=2)))
        tiles.append(chunks(a["w_out_2"][l], 512))
        gu = a["w_gate_up_2"][l].reshape(D, 2, DFF // 256, 256).transpose(0, 2, 1, 3).reshape(D, 2 * DFF)
        tiles.append(chunks(gu, 512))
        tiles.append(wide(chunks(a["w_down_2"][l], P)))
    return np.concatenate(tiles, axis=0)


def layout_cols1(a):
    out = np.zeros((DEPTH, P, NC1), np.float32)
    for l in range(DEPTH):
        o = out[l]
        o[:, C1_N1:C1_N1 + 8] = column(a["norm1_g"][l])
        o[:, C1_N2:C1_N2 + 8] = column(a["norm2_g"][l])
        o[:, C1_SUB] = a["diff_subln_g"][l]
        o[:, C1_LAM:C1_LAM + 256] = a["diff_lambda"][l].reshape(1, 256)
        o[:FH, C1_BF] = a["b_forget"][l]
        li = 0.8 - 0.6 * math.exp(-0.3 * l)
        o[:, C1_LI] = li
        o[:, C1_LI + 1] = 1.0 - li
        o[:, C1_FF:C1_FF + 64] = a["w_in"][l][:, 3072:3080].reshape(KC, P, FH).transpose(1, 0, 2).reshape(P, 64)
        o[:, C1_KEY:C1_KEY + 256] = a["sub_keys"][l].transpose(2, 0, 1).reshape(P, 256)
    return out


def layout_cols2(a):
    out = np.zeros((DEPTH, P, NC2), np.float32)
    for l in range(DEPTH):
        o = out[l]
        for at, name in ((C2_N1, "attn_norm_g_2"), (C2_N2, "ffn_norm_g_2"), (C2_QA, "q_a_norm_g_2"),
                         (C2_KVA, "kv_a_norm_g_2"), (C2_MO, "mla_out_norm_g_2"), (C2_RG, "ret_norm_g_2"),
                         (C2_RB, "ret_norm_b_2")):
            c = column(a[name][l])
            o[:, at:at + c.shape[1]] = c
        for at, name in ((C2_QG, "q_norm_g_2"), (C2_KG, "k_norm_g_2")):
            o[:, at] = a[name][l][:P]
            o[:64, at + 1] = a[name][l][P:]
        o[:, C2_KPE:] = a["w_in_2"][l][:, 512:576].reshape(KC, P, 64).transpose(1, 0, 2).reshape(P, KC * 64)
    return out


def constants1():
    k = np.zeros((P, NK1), np.float32)
    p = np.arange(P)
    k[:, K_ID:K_ID + P] = np.eye(P)
    k[:, K_FLIP:K_FLIP + P] = np.eye(P)[::-1]
    k[:, K_CEN:K_CEN + P] = np.eye(P) - 1.0 / P
    k[:, K_PM:K_PM + P] = np.roll(np.eye(P), 64, axis=1)
    k[:64, K_PR:K_PR + 64] = np.roll(np.eye(64), 32, axis=1)
    causal = np.where(p[:, None] >= p[None, :], 0.0, NEG)
    k[:, K_MASK:K_MASK + P] = causal
    k[:, K_MASK + 2 * P:K_MASK + 3 * P] = causal
    k[:, K_IOTA:K_IOTA + CAND] = np.arange(CAND)
    y = np.arange(384)
    dist = np.maximum(255 - y, 0)
    exact = BUCKETS // 2
    nf = np.maximum(dist, 1).astype(np.float32)
    large = exact + (np.log(nf / exact) / np.float32(math.log(MAX_DIST / exact)) * (BUCKETS - exact)).astype(np.int32)
    bucket = np.where(dist < exact, dist, np.minimum(large, BUCKETS - 1))
    k[:BUCKETS, K_OH:K_OH + 384] = bucket[None, :] == np.arange(BUCKETS)[:, None]
    return k


def constants2():
    k = np.zeros((P, NK2), np.float32)
    p = np.arange(P)
    for h in range(RH):
        lg = math.log(1.0 - 2.0 ** (-5.0 - h))
        for t, (m, n0, c0) in enumerate(((P, 0, 0), (P, P, T2), (16, 2 * P, 416))):
            diff = np.arange(n0, T2)[None, :] - (t * P + p[:m])[:, None]
            d = np.where(diff >= 0, np.exp(np.maximum(diff, 0) * lg), 0.0) * P ** -0.5
            k[:m, K2_D + 432 * h + c0:K2_D + 432 * h + c0 + T2 - n0] = d
    pos = np.arange(T2, dtype=np.float32)
    for dim, c, s in ((128, K2_CR, K2_SR), (64, K2_CM, K2_SM)):
        inv = (np.float32(10000.0) ** (-np.arange(0, dim, 2, dtype=np.float32) / dim)).astype(np.float32)
        ang = (pos[None, :] * inv[:, None]).astype(np.float32)
        k[:dim, c:c + T2] = np.concatenate([np.cos(ang), np.cos(ang)])
        k[:dim, s:s + T2] = np.concatenate([-np.sin(ang), np.sin(ang)])
    k[:16, K2_MASK:K2_MASK + T2] = np.where((2 * P + p[:16])[:, None] >= np.arange(T2)[None, :], 0.0, NEG)
    return k


def kernel(**inputs):
    import concourse.bacc as bacc
    from concourse.bass_utils import run_bass_kernel_spmd

    a = {k: np.asarray(v) for k, v in inputs.items()}
    feed = {
        "x": a["x"][0].T.reshape(KC, P, SEQ).transpose(1, 0, 2),
        "meta": a["meta_tokens_2"].T.reshape(KC, P, META).transpose(1, 0, 2),
        "weights": layout_stream(a),
        "cols1": layout_cols1(a),
        "cols2": layout_cols2(a),
        "final_g": column(a["final_norm_g"]),
        "rel_bias": a["rel_bias"],
        "const1": constants1(),
        "const2": constants2(),
        "expert_u": a["expert_u"],
        "expert_v": a["expert_v"],
    }
    nc = bacc.Bacc("TRN2", target_bir_lowering=False, num_devices=1)
    arrays, args = {}, []
    for name, v in feed.items():
        v = np.ascontiguousarray(v)
        arrays[f"in_{name}"] = v
        args.append(nc.dram_tensor(f"in_{name}", v.shape, mybir.dt.from_np(v.dtype), kind="ExternalInput").ap())
    args.append(nc.dram_tensor("out_x", (P, KC, SEQ), F32, kind="ExternalOutput").ap())
    program(nc, *args)
    r = run_bass_kernel_spmd(nc, [arrays], core_ids=[0])
    got = np.asarray(r.results[0]["out_x"])
    return np.ascontiguousarray(got.transpose(2, 1, 0).reshape(1, SEQ, D))
```

```python
import math
from contextlib import ExitStack

import numpy as np
import concourse.bass as bass
from concourse import mybir

ALU = mybir.AluOpType
ACT = mybir.ActivationFunctionType
AX = mybir.AxisListType
F32 = mybir.dt.float32
U32 = mybir.dt.uint32

P = 128
D = 1024
KC = D // P
SEQ = 256
META = 16
T2 = SEQ + META
DEPTH = 2
EPS = 1e-6
NEG = -1e30
BIG = 3e38

DH = 4
FH = 8
MAPS = 2 * DH + FH
BUCKETS = 32
MAX_DIST = 128
PH = 8
TOPK = 16
NEXP = 128 * 128
SLOTS = PH * TOPK
RANKS = [(0, 1, 16), (1, 1, 8), (2, 1, 5), (3, 1, 4), (4, 1, 3), (5, 3, 2), (8, 8, 1)]
CAND = sum(n * m for _, n, m in RANKS)

MH = 4
RH = 4
QKH = 192
DFF = 2816
FC = DFF // P
TILE = 4096
RING = 3
TILES1 = 18
TILES2 = 27
GB = 4
UB = 2 * GB
PAIRS = PH // 2
PART = 2 * TOPK
GROUPS = PART // GB
BANKS = 4

C1_N1, C1_N2, C1_SUB, C1_LAM, C1_BF, C1_LI, C1_FF, C1_KEY = 0, 8, 16, 17, 273, 274, 276, 340
NC1 = 596
C2_N1, C2_N2, C2_QA, C2_KVA, C2_QG, C2_KG, C2_MO, C2_RG, C2_RB, C2_KPE = 0, 8, 16, 18, 20, 22, 24, 28, 32, 36
NC2 = C2_KPE + KC * 64
K_ID, K_FLIP, K_CEN, K_PM, K_PR, K_MASK, K_IOTA, K_OH = 0, 128, 256, 384, 512, 576, 960, 1010
NK1 = K_OH + 384
K2_D, K2_CR, K2_SR, K2_CM, K2_SM, K2_MASK = 0, 1728, 2000, 2272, 2544, 2816
NK2 = K2_MASK + T2

PLAN = {
    1: (["norm1"] + [f"dq{c}" for c in range(4)] + [f"dk{c}" for c in range(4)] + ["dv0", "dv1"]
        + [f"fq{c}" for c in range(4)] + [f"fk{c}" for c in range(4)] + ["fv0", "fv1", "ff"]
        + [f"gate{c}" for c in range(16)] + [f"dnorm{h}" for h in range(DH)]
        + [f"fo{c}" for c in range(8)] + [f"do{c}" for c in range(8)] + [f"out{c}" for c in range(8)]
        + ["norm2"] + [f"hn{c}" for c in range(4)]
        + [x for t in range(4) for x in [f"wq{4 * t + c}" for c in range(4)] + [f"s{t}"]]
        + ["s6", "s7", "s4", "s5"] + [f"ft{c}" for c in range(4)]),
    "f": ["normf"],
    2: (["norm1", "cq0", "cq1", "cq2", "cq3", "kpe"] + [f"rq{c}" for c in range(4)] + ["qa", "kva", "kperm"]
        + [f"rk{c}" for c in range(4)] + [f"rv{c}" for c in range(3)] + [f"rqp{c}" for c in range(4)] + [f"rkp{c}" for c in range(4)]
        + [f"rg{c}" for c in range(4)]
        + [f"qn{c}" for c in range(4)] + [f"qr{c}" for c in range(4)] + [f"kn{c}" for c in range(4)]
        + [f"v{c}" for c in range(3)]
        + [f"qs{c}" for c in range(4)] + [f"ks{c}" for c in range(4)] + [f"qp{c}" for c in range(4)]
        + [f"rc{c}" for c in range(4)] + [f"rs{c}" for c in range(4)] + [f"ms{c}" for c in range(4)]
        + [f"out{c}" for c in range(8)] + ["norm2"]
        + [f"{x}{2 * j + i}" for j in range(11) for x in "gu" for i in range(2)]
        + [f"dn{c}" for c in range(8)]),
}
GI = {b: {n: i for i, n in enumerate(p)} for b, p in PLAN.items()}
TURNS = {b: -(-len(p) // BANKS) * BANKS for b, p in PLAN.items()}

UNIT = {2 * h + 1: h for h in range(DH)} | {2 * DH + h: DH + h for h in range(FH)}

TURN_STEPS = 29
COUNTS = {
    "w_free": (RING, TILES1, 0, TILES2), "pj_full": (0, TURNS[1], TURNS["f"], TURNS[2]),
    "s_full": (0, MAPS, 0, RH + 2 * MH), "t_done": (0, DH + FH, 0, MH), "o_full": (0, DH + FH, 0, RH + MH),
    "v_free": (UB, 2 * SLOTS, 0, 0), "f_full": (0, 2, 0, 0),
    "evac": (BANKS, TURNS[1], TURNS["f"], TURNS[2]), "sq_done": (0, 2 * KC + 1, KC, 6 + RH + MH + 2 * KC - 1),
    "e_done": (0, 2 * MAPS, 0, 3 * MH), "pt_read": (1, DH + FH, 0, MH), "o_read": (1, DH + FH, 0, RH + MH),
    "act_misc": (0, 3 + 2 * PAIRS, 0, 0), "gelu_done": (0, 2 * SLOTS // GB, 0, 0), "f_read": (0, 4, 0, 0),
    "h_done": (0, 2 * KC, 0, 2 * KC), "s_read": (2, MAPS, 0, RH + 2 * MH), "p_done": (0, MAPS, 0, MH),
    "dve_misc": (0, 271, 3, 62), "x_done": (2, KC + 4, KC, 2 * KC), "y_done": (0, DH + 8, 0, 8),
    "l_done": (0, 1, 0, 0), "c_done": (0, 1, 0, 0), "z_done": (0, 1, 0, 0), "gmax": (0, 2 * PAIRS, 0, 0),
    "idx_a": (0, 2 * PAIRS, 0, 0), "idx_b": (0, 2 * PAIRS, 0, 0), "u_free": (UB, 2 * SLOTS, 0, 0),
    "diag_done": (1, 2 * SLOTS, 0, 0),
    "small_done": (0, 0, 0, 11), "rot_done": (0, 0, 0, 2 * RH + 2 * MH), "b2_act": (0, 0, 0, FC),
    "rstd": (0, 2 + DH, 1, 20),
    "cols_full": (0, 16, 0, 16),
}


def program(nc, x_in, meta_in, ws, c1_in, c2_in, fin_g, rel, k1_in, k2_in, eu, ev, out):
    with ExitStack() as ctx:
        def sb(name, shape, dt=F32):
            return ctx.enter_context(nc.sbuf_tensor(name, shape, dt))

        def bank(name):
            return ctx.enter_context(nc.psum_tensor(name, [P, 512], F32))

        def sem(name):
            return ctx.enter_context(nc.semaphore(name))

        wring = sb("wring", [P, RING, TILE])
        area = sb("area", [P, 16384])
        area2 = sb("area2", [P, 10752])
        xT = sb("xT", [P, KC, T2])
        hT = sb("hT", [P, KC, T2])
        sq = sb("sq", [P, KC, T2])
        ms = sb("ms", [P, 4, T2])
        rstd = sb("rstd", [P, 8, T2])
        cols = sb("cols", [P, max(NC1, NC2)])
        fing = sb("fing", [P, KC])
        relb = sb("relb", [BUCKETS, DH])
        kst = sb("kst", [P, K_OH])
        ones = sb("ones", [P, P])
        eps = sb("eps", [P, 3])
        nsel = sb("nsel", [FH, FH])
        bias = sb("bias", [P, DH, 384])
        nmax = sb("nmax", [P, 2, 3])
        esum = sb("esum", [P, 2, 3])
        erec = sb("erec", [P, 2, 3])
        lam = sb("lam", [P, 8])
        loff = sb("loff", [P, 1])
        junk = sb("junk", [P, 128])
        k2st = area[:, 16384 - NK2:16384]

        def part(buf, at, *shape):
            n = math.prod(shape)
            v = buf[:, at:at + n]
            names = "abc"[:len(shape)]
            if len(shape) == 1:
                return v
            return v.rearrange(f"p ({' '.join(names)}) -> p {' '.join(names)}",
                               **{k: s for k, s in zip(names, shape)})

        ident = kst[:, K_ID:K_ID + P]
        flip = kst[:, K_FLIP:K_FLIP + P]
        center = kst[:, K_CEN:K_CEN + P]
        swap128 = kst[:, K_PM:K_PM + P]
        swap64 = kst[0:64, K_PR:K_PR + 64]
        mask = kst[:, K_MASK:K_MASK + 384]
        iota = kst[:, K_IOTA:K_IOTA + CAND]

        dqT, dkT, fqT, fkT = (part(area, 1024 * i, 4, SEQ) for i in range(4))
        dv, fv = (part(area, 4096 + 1024 * i, 2, 512) for i in range(2))
        gate = part(area, 6144, 16, SEQ)
        doT, foT = part(area, 10240, 8, SEQ), part(area, 12288, 8, SEQ)
        ydT, yfT = part(area, 14336, 4, SEQ), part(area, 15360, 4, SEQ)
        urow, vrow = part(area, 0, UB, D), part(area, UB * D, UB, D)
        mgT = part(area2, 0, 8, SEQ)
        qT = part(area2, 0, 16, SEQ)
        keys_at = lambda n: 2048 + 512 * (2 * PAIRS - 1 - n)
        h2n = part(area2, 6144, 2, D)
        oTmp = part(area2, 8192, 8, SEQ)
        eq = part(area2, 8192, PART, CAND)
        cnd, cidx = part(area2, 9792, 2, CAND), part(area2, 9792 + 2 * CAND, 2, CAND)
        topv, topf = part(area2, 10000, 4, TOPK), part(area2, 10064, 4, TOPK)
        topi = area2[:, 10128:10192].bitcast(U32).rearrange("p (a k) -> p a k", k=TOPK)
        bestv, bestf = part(area2, 10192, 2, TOPK), part(area2, 10224, 2, TOPK)
        bestp = area2[:, 10256:10288].bitcast(U32).rearrange("p (a k) -> p a k", k=TOPK)
        gexp = part(area2, 10288, 2, TOPK)
        gnext, gates = part(area2, 10320, 2, TOPK), area2[:, 10352:10384]
        gsum = part(area2, 10384, 2, 2)
        idxf = sb("idxf", [P, PART])
        idx = sb("idx", [P, PART], U32)
        dots = sb("dots", [P, 2, GB])
        gl = sb("gl", [P, 2, GB])
        wgt = sb("wgt", [P, 2, GB])
        sqflat = sq[:, :, :].rearrange("p c t -> p (c t)")
        work = part(sqflat, 0, 4, P)
        diag = part(sqflat, 512, UB, P)
        fn = part(area2, 0, D)
        fT = (part(area2, D, 8, P), part(hT[:, :, :].rearrange("p c t -> p (c t)"), 0, 8, P))

        zeros = eps[:, 2:3].to_broadcast([P, 512])
        nl, ex, pr, pt = (part(area2, 4352 + 1312 * i, 2, n) for i, n in enumerate((656, 656, 656, 432)))
        fox = area2[0:FH, 9152:9152 + 6 * SEQ].rearrange("p (a n) -> p a n", a=6)
        onehot = area[0:BUCKETS, 0:384]
        gvec = area2[0:DH, 0:384]
        cosR, sinR = (k2st[:, c:c + T2] for c in (K2_CR, K2_SR))
        cosM, sinM = (k2st[0:64, c:c + T2] for c in (K2_CM, K2_SM))

        cq = part(area, 0, 4, T2)
        kpe, kpg, kro = (part(area, 1088 + T2 * i, T2) for i in range(3))
        rq, rk = part(area, 1904, 4, T2), part(area, 2992, 4, T2)
        rv, v2 = part(area, 4080, 3, 512), part(area, 11056, 3, 512)
        rgt, rgr = part(area, 5616, 4, T2), part(area, 6704, 4, T2)
        qn, qr, kn = (part(area, 7792 + 1088 * i, 4, T2) for i in range(3))
        kr, ro, mo = rk, rq, qn
        yT, tmpR = part(area2, 0, 8, T2), part(area2, 0, 8, T2)
        tmpP = part(area2, 2176, 5, T2)
        actT = part(area2, 4352, FC, T2)
        oTmp2 = part(area, 0, 8, T2)
        gbuf = part(area, 4352, 2, 6, T2)

        PJ = [bank(f"pj{i}") for i in range(BANKS)]
        S = [bank("s0"), bank("s1")]
        PT = bank("ptb")
        O = bank("ob")

        N = {n: sem(n) for n in COUNTS}
        w_full = [sem(f"w_full{i}") for i in range(RING)]
        u_full = [sem(f"u_full{i}") for i in range(UB)]
        v_full = [sem(f"v_full{i}") for i in range(UB)]
        const_full, const2_full = sem("const_full"), sem("const2_full")
        memset_done, setup_dve = sem("memset_done"), sem("setup_dve")
        setup_pe, setup_act = sem("setup_pe"), sem("setup_act")
        scratch_out, scratch_in, out_full = sem("scratch_out"), sem("scratch_in"), sem("out_full")
        held = {e: sem(f"held_{e}") for e in ("pe", "act", "dve", "pool")}

        class Layer:

            def __init__(self, block, l):
                self.block, self.l, self.n = block, l, {}
                self.g = 0
                self.j, self.per = 0, {}

            def at(self, name, k):
                pre, a, f, b = COUNTS[name]
                if self.block == 1:
                    v = self.l * a + (pre + k)
                    return v + self.j * self.per[name] if self.per else v
                if self.block == "f":
                    return pre + DEPTH * a + k
                return self.l * b + (pre + DEPTH * a + f + k)

            def turns(self, eng, n, per, body):
                before = dict(self.n)
                with eng.Fori(0, n) as j:
                    self.j, self.per = j, per
                    body(j)
                self.j, self.per = 0, {}
                for name, k in self.n.items():
                    once = k - before.get(name, 0)
                    if once:
                        assert once == per[name], (name, once)
                        self.n[name] = k + (n - 1) * once

            def inc(self, ins, name, by=1):
                ins.then_inc(N[name], by)
                self.n[name] = self.n.get(name, 0) + by

            def wait(self, eng, name, k):
                eng.wait_ge(N[name], self.at(name, k))

            def hold(self, eng, who, name, k):
                eng.wait_ge(N[name], self.at(name, k))
                eng.sem_inc(held[who], 1)

            def evacuated(self, eng, group):
                self.wait(eng, "evac", GI[self.block][group] + 1)

            def check(self, names):
                i = {1: 1, "f": 2, 2: 3}[self.block]
                for n in names:
                    if self.n.get(n, 0) != COUNTS[n][i]:
                        print("COUNT", self.block, n, self.n.get(n, 0), "declared", COUNTS[n][i])
                        assert False, n

        scratch = nc.dram_tensor("bias_scratch", [DH, 384], F32, kind="Internal")
        block = ctx.enter_context(nc.Block())

        @block.sync
        def _(sp):
            sp.dma_start(kst[:], k1_in[:, 0:K_OH]).then_inc(const_full, 16)
            sp.dma_start(onehot, k1_in[0:BUCKETS, K_OH:NK1]).then_inc(const_full, 16)
            sp.dma_start(relb[:], rel).then_inc(const_full, 16)
            sp.dma_start(xT[:, :, META:T2], x_in).then_inc(const_full, 16)
            sp.dma_start(xT[:, :, 0:META], meta_in).then_inc(const_full, 16)
            sp.dma_start(fing[:], fin_g).then_inc(const_full, 16)
            with sp.Fori(0, DEPTH * (TILES1 + TILES2) // RING) as r:
                for i in range(RING):
                    sp.wait_ge(N["w_free"], r * RING + (i + 1))
                    sp.dma_start(wring[:, i, :], ws[r * RING + i, :, :]).then_inc(w_full[i], 16)
            before, first, final, second = COUNTS["x_done"]
            sp.wait_ge(N["x_done"], before + DEPTH * (first + second) + final)
            sp.dma_start(out, xT[:, :, META:T2]).then_inc(out_full, 16)
            sp.wait_ge(out_full, 16)

        def tile_ready(eng, L, t):
            if L.block == 1:
                eng.wait_ge(w_full[t % RING], L.l * (16 * TILES1 // RING) + 16 * (t // RING + 1))
            else:
                eng.wait_ge(w_full[t % RING], L.l * (16 * TILES2 // RING)
                            + 16 * (DEPTH * TILES1 // RING + t // RING + 1))
            return wring[:, t % RING, :]

        TX = slice(META, T2)
        ATILES = ((0, P), (P, P), (2 * P, T2 - 2 * P))

        @block.tensor
        def _(pe):
            pe.sem_inc(N["w_free"], 1)
            pe.sem_inc(N["v_free"], UB)
            pe.wait_ge(const_full, 96)
            pe.matmul(PJ[0][0:DH, 0:384], relb[:], onehot,
                      start=True, stop=True).then_inc(setup_pe, 1)
            pe.wait_ge(scratch_in, 16)
            pe.sem_inc(N["w_free"], RING - 1)
            pe.wait_ge(setup_act, 1)
            for h in range(DH):
                m = pe.matmul(S[h // 2][:, 256 * (h % 2):256 * (h % 2) + 256], flip, doT[:, h, :], start=True, stop=True)
            m.then_inc(setup_pe, 1)
            pe.wait_ge(memset_done, 1)

            class Products(Layer):
                owed = False
                arriving = None

                def mm(self, out, lhs, rhs, start, stop, last=False):
                    m = pe.matmul(out, lhs, rhs, start=start, stop=stop)
                    if self.owed and not last:
                        self.inc(m, "w_free")
                        self.owed = False
                    return m

                def group(self, name):
                    assert PLAN[self.block][self.g] == name, (PLAN[self.block][self.g], name)
                    pe.wait_ge(N["evac"], self.at("evac", self.g + 1 - BANKS))
                    b = PJ[self.g % BANKS]
                    self.g += 1
                    return b

                def stats(self, name, squares, n, done=None):
                    b = self.group(name)
                    for c, s in enumerate(squares):
                        if done is not None:
                            pe.wait_ge(N["sq_done"], self.at("sq_done", done + c + 1))
                        m = self.mm(b[:, 0:n], ones[0:s.shape[0], :], s, c == 0, c == len(squares) - 1,
                                    last=c == len(squares) - 1)
                    self.inc(m, "pj_full")

                def chunk(self, name, w, m0, rhs, kcs, n, m=P, order=None):
                    b = self.group(name)
                    for i, k in enumerate(order or range(kcs)):
                        if self.arriving:
                            name, before = self.arriving
                            pe.wait_ge(N[name], self.at(name, before + i + 1))
                        p = self.mm(b[0:m, 0:n], w[:, k, m0:m0 + m], rhs(k), i == 0, i == kcs - 1, last=i == kcs - 1)
                    self.inc(p, "pj_full")
                    self.arriving = None

                def tokens(self, name, w, n0, act, kcs, t0, m):
                    b = self.group(name)
                    for k in range(kcs):
                        i = self.mm(b[0:m, :], act(k)[:, t0:t0 + m], w[:, k, n0:n0 + 512], k == 0, k == kcs - 1,
                                    last=k == kcs - 1)
                    self.inc(i, "pj_full")

                def pad(self):
                    n = TURNS[self.block] - len(PLAN[self.block])
                    assert self.g == len(PLAN[self.block]) and not self.owed
                    if n:
                        pe.wait_ge(N["pj_full"], self.at("pj_full", self.n["pj_full"]))
                        pe.sem_inc(N["pj_full"], n)
                        self.n["pj_full"] += n

            def block1(l):
                L = Products(1, l)
                keys = cols[:, C1_KEY:C1_KEY + 256].rearrange("p (a n) -> p a n", a=2)
                hx = lambda k: hT[:, k, TX]

                def feature_tile(t, names):
                    w = tile_ready(pe, L, t).rearrange("p (k n) -> p k n", k=KC)
                    for m, n in enumerate(names):
                        L.chunk(n, w, m * P, hx, KC, SEQ)
                    L.owed = True

                def token_tile(t, name):
                    w = tile_ready(pe, L, t).rearrange("p (k n) -> p k n", k=KC)
                    for tt in range(2):
                        L.tokens(f"{name}{tt}", w, 0, lambda k: hT[:, k, :], KC, META + tt * P, P)
                    L.owed = True

                L.stats("norm1", [sq[:, c, TX] for c in range(KC)], SEQ, done=0)
                L.arriving = "h_done", 0
                feature_tile(0, [f"dq{c}" for c in range(4)])
                feature_tile(1, [f"dk{c}" for c in range(4)])
                token_tile(2, "dv")
                feature_tile(3, [f"fq{c}" for c in range(4)])
                feature_tile(4, [f"fk{c}" for c in range(4)])
                token_tile(5, "fv")
                pe.wait_ge(N["cols_full"], L.at("cols_full", 16))
                L.chunk("ff", cols[:, C1_FF:C1_FF + KC * FH].rearrange("p (k n) -> p k n", k=KC), 0, hx, KC, SEQ, m=FH)

                def scores(i):
                    fo = i >= 2 * DH
                    if i == 0:
                        L.evacuated(pe, "dk3")
                    if i == 2 * DH:
                        L.evacuated(pe, "fk3")
                        pe.wait_ge(N["c_done"], L.at("c_done", 1))
                    pe.wait_ge(N["s_read"], L.at("s_read", i - 1))
                    j = i - 2 * DH if fo else i
                    q, k = (fqT, fkT) if fo else (dqT, dkT)
                    r = slice(64 * (j % 2), 64 * (j % 2) + 64)
                    for qt, (c0, n) in enumerate(((0, P), (P, 2 * P))):
                        o = S[i % 2][:, c0:c0 + n]
                        m = pe.matmul(o, q[r, j // 2, qt * P:(qt + 1) * P], k[r, j // 2, 0:n], start=True, stop=not fo)
                        if fo:
                            pe.matmul(o, fox[:, 5, qt * P:(qt + 1) * P], ident[0:FH, j:j + 1].to_broadcast([FH, n]),
                                      start=False, stop=False)
                            m = pe.matmul(o, nsel[:, j:j + 1].to_broadcast([FH, P]), fox[:, 5, 0:n], start=False, stop=True)
                    L.inc(m, "s_full")

                def turn(u, i):
                    pe.wait_ge(N["p_done"], L.at("p_done", i + 1))
                    pe.wait_ge(N["pt_read"], L.at("pt_read", u))
                    for c in range(3):
                        m = pe.transpose(PT[:, c * P:(c + 1) * P], pr[:, u % 2, c * P:(c + 1) * P], ident)
                    L.inc(m, "t_done")

                def values(u):
                    if u == 0:
                        L.evacuated(pe, "fv1")
                    pe.wait_ge(N["pt_read"], L.at("pt_read", u + 1))
                    pe.wait_ge(N["o_read"], L.at("o_read", u))
                    v, c = (dv, u) if u < DH else (fv, (u - DH) // 2)
                    pe.matmul(O[:, 0:SEQ], v[:, 0, c * P:(c + 1) * P], pt[:, u % 2, 0:SEQ], start=True, stop=False)
                    m = pe.matmul(O[:, P:SEQ], v[:, 1, c * P:(c + 1) * P], pt[:, u % 2, SEQ:384], start=False, stop=True)
                    L.inc(m, "o_full")

                for i in range(MAPS + 2):
                    if i < MAPS:
                        scores(i)
                        if i % 4 == 0:
                            w = tile_ready(pe, L, 6 + i // 4).rearrange("p (k n) -> p k n", k=KC)
                        L.chunk(f"gate{i}", w, (i % 4) * P, hx, KC, SEQ)
                        if i % 4 == 3:
                            L.owed = True
                    if i - 1 in UNIT:
                        turn(UNIT[i - 1], i - 1)
                    if i - 2 in UNIT:
                        values(UNIT[i - 2])

                pe.wait_ge(N["sq_done"], L.at("sq_done", KC + 1))
                for h in range(DH):
                    L.stats(f"dnorm{h}", [sq[:, h, TX]], SEQ)
                w = tile_ready(pe, L, 10).rearrange("p (k n) -> p k n", k=4)
                pe.wait_ge(N["o_read"], L.at("o_read", DH + FH))
                for c in range(8):
                    L.chunk(f"fo{c}", w, c * P, lambda k: yfT[:, k, :], 4, SEQ)
                L.owed = True
                w = tile_ready(pe, L, 11).rearrange("p (k n) -> p k n", k=4)
                L.arriving = "y_done", 0
                for c in range(8):
                    L.chunk(f"do{c}", w, c * P, lambda k: ydT[:, k, :], 4, SEQ)
                L.owed = True
                L.arriving = "y_done", DH
                for t in range(2):
                    w = tile_ready(pe, L, 12 + t).rearrange("p (k n) -> p k n", k=KC)
                    for c in range(4):
                        L.chunk(f"out{4 * t + c}", w, c * P, lambda k: mgT[:, k, :], KC, SEQ)
                    L.owed = True

                L.stats("norm2", [sq[:, c, TX] for c in range(KC)], SEQ, done=KC + 1)
                for tt in range(2):
                    for hf in range(2):
                        b = L.group(f"hn{2 * tt + hf}")
                        for c in range(4):
                            if tt == 0:
                                pe.wait_ge(N["h_done"], L.at("h_done", KC + 4 * hf + c + 1))
                            m = pe.transpose(b[:, c * P:(c + 1) * P],
                                             hT[:, 4 * hf + c, META + tt * P:META + (tt + 1) * P], ident)
                        L.inc(m, "pj_full")


                def key_scores(k):
                    tt, g = k // PAIRS, k % PAIRS
                    L.hold(pe, "pe", "evac", GI[1][f"wq{4 * g + 3}"] + 1)
                    b = L.group(f"s{k}")
                    for c in range(4):
                        hp = 4 * g + c
                        m = L.mm(b[:, c * P:(c + 1) * P], qT[:, hp, tt * P:(tt + 1) * P], keys[:, hp % 2, :],
                                 True, True, last=c == 3)
                    L.inc(m, "pj_full")

                for t in range(4):
                    feature_tile(14 + t, [f"wq{4 * t + c}" for c in range(4)])
                    key_scores(t)
                for k in (6, 7, 4, 5):
                    key_scores(k)
                for tt in range(2):
                    if tt:
                        pe.wait_ge(N["f_read"], L.at("f_read", 2))
                    for n in range(2):
                        pe.matmul(S[n][:], ident, zeros, start=True, stop=False)
                    with pe.Fori(0, SLOTS // (8 * GB)) as j:
                        for g in range(8):
                            for i in range(GB):
                                b = GB * (g % 2) + i
                                pe.wait_ge(N["diag_done"], L.at("diag_done", tt * SLOTS + GB * g + i + 1) + j * (8 * GB))
                                pe.wait_ge(v_full[b], L.l * (32 * SLOTS // UB) + j * 64
                                           + 16 * (tt * SLOTS // UB + g // 2 + 1))
                                for n in range(2):
                                    m = pe.matmul(S[n][:], diag[:, b, :], vrow[:, b, n * 512:(n + 1) * 512],
                                                  start=False, stop=False)
                                m.then_inc(N["v_free"], 1)
                    L.n["v_free"] = L.n.get("v_free", 0) + SLOTS
                    for n in range(2):
                        m = pe.matmul(S[n][:], ident, zeros, start=False, stop=True)
                    L.inc(m, "f_full")
                    for hf in range(2):
                        pe.wait_ge(N["f_read"], L.at("f_read", 2 * tt + hf + 1))
                        b = L.group(f"ft{2 * tt + hf}")
                        for c in range(4):
                            m = pe.transpose(b[:, c * P:(c + 1) * P], fn[:, (4 * hf + c) * P:(4 * hf + c + 1) * P], ident)
                        L.inc(m, "pj_full")
                L.pad()
                L.check(["pj_full", "w_free", "s_full", "t_done", "o_full", "v_free", "f_full"])

            def block2(l):
                L = Products(2, l)
                hx = lambda k: hT[:, k, :]

                def feature_tile(t, names):
                    w = tile_ready(pe, L, t).rearrange("p (k n) -> p k n", k=KC)
                    for m, n in enumerate(names):
                        L.chunk(n, w, m * P, hx, KC, T2)
                    L.owed = True

                L.stats("norm1", [sq[:, c, :] for c in range(KC)], T2, done=0)
                L.arriving = "h_done", 0
                feature_tile(0, [f"cq{c}" for c in range(4)])
                pe.wait_ge(N["cols_full"], L.at("cols_full", 16))
                L.chunk("kpe", cols[:, C2_KPE:C2_KPE + KC * 64].rearrange("p (k n) -> p k n", k=KC), 0, hx, KC, T2, m=64)
                feature_tile(1, [f"rq{c}" for c in range(4)])
                pe.wait_ge(N["sq_done"], L.at("sq_done", KC + 1))
                L.stats("qa", [sq[:, c, :] for c in (0, 1)], T2)
                L.stats("kva", [sq[:, c, :] for c in (2, 3)], T2)

                def swap(name, perm, m, src):
                    b = L.group(name)
                    pe.sem_inc(held["pe"], 1)
                    i = L.mm(b[0:m, 0:T2], perm, src, True, True, last=True)
                    L.inc(i, "pj_full")

                pe.wait_ge(N["small_done"], L.at("small_done", 3))
                swap("kperm", swap64, 64, kpg[0:64, :])
                feature_tile(2, [f"rk{c}" for c in range(4)])
                w = tile_ready(pe, L, 3).rearrange("p (k n) -> p k n", k=KC)
                for t, (t0, m) in enumerate(ATILES):
                    L.tokens(f"rv{t}", w, 0, hx, KC, t0, m)
                L.owed = True
                L.evacuated(pe, "rk3")
                for h in range(RH):
                    swap(f"rqp{h}", swap128, P, rq[:, h, :])
                for h in range(RH):
                    swap(f"rkp{h}", swap128, P, rk[:, h, :])
                feature_tile(4, [f"rg{c}" for c in range(4)])
                w5 = tile_ready(pe, L, 5)
                wq = w5[:, 0:1536].rearrange("p (k n) -> p k n", k=2)
                wkv = w5[:, 1536:3584].rearrange("p (k n) -> p k n", k=2)
                pe.wait_ge(N["small_done"], L.at("small_done", 7))
                for h in range(MH):
                    L.chunk(f"qn{h}", wq, h * P, lambda k: cq[:, k, :], 2, T2)
                for h in range(MH):
                    L.chunk(f"qr{h}", wq, 512 + h * 64, lambda k: cq[:, k, :], 2, T2, m=64)
                for h in range(MH):
                    L.chunk(f"kn{h}", wkv, h * P, lambda k: cq[:, 2 + k, :], 2, T2)
                for t, (t0, m) in enumerate(ATILES):
                    L.tokens(f"v{t}", wkv, 512, lambda k: cq[:, 2 + k, :], 2, t0, m)
                L.owed = True

                KTILES = ((0, P, 0, 0), (1, P, P, T2), (2, T2 - 2 * P, 2 * P, 2 * T2 - P))

                def ret_scores(h):
                    pe.wait_ge(N["rot_done"], L.at("rot_done", 2 * (h + 1)))
                    pe.wait_ge(N["s_read"], L.at("s_read", h - 1))
                    for t, m, n0, c0 in KTILES:
                        i = L.mm(S[h % 2][0:m, c0:c0 + T2 - n0], rk[:, h, t * P:t * P + m], rq[:, h, n0:T2], True, True,
                                 last=t == 2)
                    L.inc(i, "s_full")

                def sums(u, buf, val, h):
                    pe.wait_ge(N["o_read"], L.at("o_read", u))
                    for t, m, n0, c0 in KTILES:
                        i = pe.matmul(O[:, n0:T2], val[0:m, t, h * P:(h + 1) * P], buf[0:m, c0:c0 + T2 - n0],
                                      start=t == 0, stop=t == 2)
                    L.inc(i, "o_full")

                for h in range(RH + 1):
                    if h < RH:
                        ret_scores(h)
                    if h:
                        pe.wait_ge(N["s_read"], L.at("s_read", h))
                        sums(h - 1, pr[:, (h - 1) % 2, :], rv, h - 1)

                pe.wait_ge(N["sq_done"], L.at("sq_done", KC + 3))
                for h in range(MH):
                    L.stats(f"qs{h}", [sq[:, h, :], sq[0:64, 4 + h, :]], T2)
                pe.wait_ge(N["sq_done"], L.at("sq_done", KC + 5))
                for h in range(MH):
                    L.stats(f"ks{h}", [hT[:, h, :], hT[0:64, 4, :]], T2)
                for h in range(MH):
                    pe.wait_ge(N["small_done"], L.at("small_done", 7 + h + 1))
                    swap(f"qp{h}", swap64, 64, qr[0:64, h, :])

                def mla_scores(h):
                    pe.wait_ge(N["rot_done"], L.at("rot_done", 2 * RH + 2 * (h + 1)))
                    use = RH + 2 * h
                    for part_, regions in enumerate((((0, P, 0, P), (P, P, P, 2 * P)), ((2 * P, T2 - 2 * P, 0, T2),))):
                        pe.wait_ge(N["s_read"], L.at("s_read", use + part_ - 1))
                        for q0, m, c0, n in regions:
                            o = S[(use + part_) % 2][0:m, c0:c0 + n]
                            pe.matmul(o, qn[:, h, q0:q0 + m], kn[:, h, 0:n], start=True, stop=False)
                            i = pe.matmul(o, qr[0:64, h, q0:q0 + m], kr[0:64, h, 0:n], start=False, stop=True)
                        L.inc(i, "s_full")

                def mla_turn(h):
                    pe.wait_ge(N["p_done"], L.at("p_done", h + 1))
                    pe.wait_ge(N["pt_read"], L.at("pt_read", h))
                    p = pr[:, h % 2, :]
                    pe.transpose(PT[:, 0:P], p[:, 0:P], ident)
                    pe.transpose(PT[:, P:2 * P], p[:, P:2 * P], ident)
                    pe.transpose(PT[:, T2:T2 + P], p[:, 2 * P:3 * P], ident)
                    pe.transpose(PT[:, 2 * P:T2], p[0:16, 384:384 + P], ident[0:16, 0:16])
                    pe.transpose(PT[:, T2 + P:T2 + P + 16], p[0:16, 384 + P:384 + 2 * P], ident[0:16, 0:16])
                    i = pe.transpose(PT[0:16, 2 * T2 - P:2 * T2 - P + 16], p[0:16, 384 + 2 * P:384 + T2], ident[0:16, 0:16])
                    L.inc(i, "t_done")

                pe.wait_ge(N["o_read"], L.at("o_read", RH))
                for h in range(MH + 1):
                    if h < MH:
                        mla_scores(h)
                        b = L.group(f"rc{h}")
                        L.inc(L.mm(b[:, 0:T2], center, ro[:, h, :], True, True, last=True), "pj_full")
                    if h == MH:
                        for r in range(RH):
                            pe.wait_ge(N["sq_done"], L.at("sq_done", KC + 5 + max(2 * r, 1)))
                            L.stats(f"rs{r}", [sq[:, r, :]], T2)
                    if h:
                        mla_turn(h - 1)
                        pe.wait_ge(N["pt_read"], L.at("pt_read", h))
                        sums(RH + h - 1, pt[:, (h - 1) % 2, :], v2, h - 1)

                for h in range(MH):
                    pe.wait_ge(N["sq_done"], L.at("sq_done", KC + 5 + min(2 * h + 3, RH + MH)))
                    L.stats(f"ms{h}", [sq[:, 4 + h, :]], T2)
                L.arriving = "y_done", 0
                for t in range(2):
                    w = tile_ready(pe, L, 6 + t).rearrange("p (k n) -> p k n", k=KC)
                    for c in range(4):
                        L.chunk(f"out{4 * t + c}", w, c * P, lambda k: yT[:, k, :], KC, T2, order=(4, 5, 6, 7, 0, 1, 2, 3))
                    L.owed = True
                L.stats("norm2", [sq[:, c, :] for c in range(KC)], T2, done=KC + 5 + RH + MH)
                L.arriving = "h_done", KC
                for j in range(11):
                    feature_tile(8 + j, [f"g{2 * j}", f"g{2 * j + 1}", f"u{2 * j}", f"u{2 * j + 1}"])
                L.arriving = "b2_act", 0
                for c in range(8):
                    w = tile_ready(pe, L, 19 + c)[:, 0:FC * P].rearrange("p (k n) -> p k n", k=FC)
                    L.chunk(f"dn{c}", w, 0, lambda k: actT[:, k, :], FC, T2)
                    L.owed = True
                L.owed = False
                pe.wait_ge(N["pj_full"], L.at("pj_full", L.n["pj_full"]))
                pe.sem_inc(N["w_free"], 1)
                L.n["w_free"] += 1
                L.pad()
                L.check(["pj_full", "w_free", "s_full", "t_done", "o_full", "v_free", "f_full"])

            with pe.Fori(0, DEPTH) as l:
                block1(l)
            L = Products("f", 0)
            L.stats("normf", [sq[:, c, TX] for c in range(KC)], SEQ, done=0)
            L.pad()
            with pe.Fori(0, DEPTH) as l:
                block2(l)

        @block.scalar
        def _(act):
            act.sem_inc(N["evac"], BANKS)
            act.sem_inc(N["pt_read"], 1)
            act.sem_inc(N["o_read"], 1)
            act.wait_ge(memset_done, 1)
            act.wait_ge(setup_pe, 1)
            act.activation(gvec, PJ[0][0:DH, 0:384], ACT.Copy).then_inc(setup_act, 1)
            act.wait_ge(setup_act, 1)
            act.dma_start(scratch[:], gvec).then_inc(scratch_out, 16)
            act.wait_ge(scratch_out, 16)
            act.dma_start(doT[:, 0:DH, :], bass.AP(tensor=scratch, offset=0, ap=[[1, P], [384, DH], [1, 256]]))\
               .then_inc(scratch_in, 16)

            class Copies(Layer):
                def src(self, name):
                    assert PLAN[self.block][self.g] == name, (PLAN[self.block][self.g], name)
                    act.wait_ge(N["pj_full"], self.at("pj_full", self.g + 1))
                    b = PJ[self.g % BANKS]
                    self.g += 1
                    return b

                def out(self, name, dst, n, m0=0, m=P, scale=1.0):
                    b = self.src(name)[m0:m0 + m, 0:n]
                    if len(dst.shape) == 3:
                        b = b.rearrange("p (a n) -> p a n", a=dst.shape[1])
                    self.inc(act.activation(dst, b, ACT.Copy, scale=scale), "evac")

                def mean(self, name, dst, n, width):
                    b = self.src(name)
                    if width == D:
                        act.activation(rstd[:, 7, 0:n], b[:, 0:n], ACT.Identity, scale=1.0 / width, bias=eps[:, 0:1])
                    self.inc(act.activation(dst, b[:, 0:n], ACT.Sqrt, scale=1.0 / width, bias=eps[:, 0:1]), "evac")

                def square(self, dst, src):
                    self.inc(act.activation(dst, src, ACT.Square), "sq_done")

                def square_all(self):
                    for c in range(KC):
                        act.wait_ge(N["x_done"], self.at("x_done", -1 if c < KC // 2 else 0))
                        self.square(sq[:, c, TX], xT[:, c, TX])

                def pad(self):
                    n = TURNS[self.block] - len(PLAN[self.block])
                    assert self.g == len(PLAN[self.block])
                    if n:
                        act.wait_ge(N["evac"], self.at("evac", self.n["evac"]))
                        act.sem_inc(N["evac"], n)
                        self.n["evac"] += n

            def block1(l):
                L = Copies(1, l)
                L.square_all()
                L.mean("norm1", ms[:, 0, 0:SEQ], SEQ, D)
                for c in range(4):
                    L.out(f"dq{c}", dqT[:, c, :], SEQ, scale=0.125)
                for c in range(4):
                    L.out(f"dk{c}", dkT[:, c, :], SEQ)
                for c in range(2):
                    L.out(f"dv{c}", dv[:, c, :], 512)
                for c in range(4):
                    L.out(f"fq{c}", fqT[:, c, :], SEQ, scale=0.125)
                for c in range(4):
                    L.out(f"fk{c}", fkT[:, c, :], SEQ)
                for c in range(2):
                    L.out(f"fv{c}", fv[:, c, :], 512)
                act.wait_ge(N["cols_full"], L.at("cols_full", 16))
                b = L.src("ff")
                L.inc(act.activation(fox[:, 0, :], b[0:FH, 0:SEQ], ACT.Identity, bias=cols[0:FH, C1_BF:C1_BF + 1]), "evac")
                act.wait_ge(N["l_done"], L.at("l_done", 1))
                L.inc(act.activation(lam[:, 2:4], lam[:, 0:2], ACT.Exp), "act_misc")
                act.wait_ge(N["z_done"], L.at("z_done", 1))
                L.inc(act.activation(fox[:, 3, :], fox[:, 2, :], ACT.Exp, scale=-1.0), "act_misc")
                act.wait_ge(N["act_misc"], L.at("act_misc", 2))
                L.inc(act.activation(fox[:, 4, :], fox[:, 3, :], ACT.Ln, bias=eps[0:FH, 1:2]), "act_misc")

                def exps(i):
                    act.wait_ge(N["s_read"], L.at("s_read", i + 1))
                    if i >= 2:
                        act.wait_ge(N["p_done"], L.at("p_done", i - 1))
                    for r, (c0, n) in enumerate(((0, P), (P, 2 * P))):
                        L.inc(act.activation(ex[:, i % 2, c0:c0 + n], nl[:, i % 2, c0:c0 + n], ACT.Exp, scale=-1.0,
                                             bias=nmax[:, i % 2, r:r + 1], accum_out=esum[:, i % 2, r:r + 1]), "e_done")

                def turned(u):
                    act.wait_ge(N["t_done"], L.at("t_done", u + 1))
                    if u >= 2:
                        act.wait_ge(N["o_full"], L.at("o_full", u - 1))
                    L.inc(act.activation(pt[:, u % 2, 0:384], PT[:, 0:384], ACT.Copy), "pt_read")

                def outputs(u):
                    act.wait_ge(N["o_full"], L.at("o_full", u + 1))
                    if u < DH:
                        i = act.activation(ydT[:, u, :], O[:, 0:SEQ], ACT.Copy)
                    else:
                        r = slice(64 * (u % 2), 64 * (u % 2) + 64)
                        i = act.activation(yfT[r, (u - DH) // 2, :], O[r, 0:SEQ], ACT.Copy)
                    L.inc(i, "o_read")

                for i in range(MAPS + 2):
                    if i < MAPS:
                        exps(i)
                        b = L.src(f"gate{i}")
                        L.inc(act.activation(gate[:, i, :], b[:, 0:SEQ], ACT.Tanh, scale=0.5), "evac")
                    if i - 1 in UNIT:
                        turned(UNIT[i - 1])
                    if i - 2 in UNIT:
                        outputs(UNIT[i - 2])
                        if UNIT[i - 2] == DH - 1:
                            act.wait_ge(N["o_read"], L.at("o_read", DH))
                            L.square(sq[:, 0:DH, TX], ydT)
                for h in range(DH):
                    L.mean(f"dnorm{h}", ms[:, h, 0:SEQ], SEQ, P)
                for c in range(8):
                    L.out(f"fo{c}", foT[:, c, :], SEQ, scale=0.5)
                for c in range(8):
                    L.out(f"do{c}", doT[:, c, :], SEQ, scale=0.5)
                def square_chunk(c):
                    act.wait_ge(N["x_done"], L.at("x_done", c + 1))
                    L.square(sq[:, c, TX], xT[:, c, TX])

                for c in range(8):
                    L.out(f"out{c}", oTmp[:, c, :], SEQ)
                    if c:
                        square_chunk(c - 1)
                square_chunk(7)
                L.mean("norm2", ms[:, 0, 0:SEQ], SEQ, D)
                for c in range(4):
                    L.out(f"hn{c}", h2n[:, c // 2, (c % 2) * 512:(c % 2 + 1) * 512], 512)

                def key_scores(k):
                    L.out(f"s{k}", area2[:, keys_at(k):keys_at(k) + 512], 512)

                def gate_exps(n):
                    act.wait_ge(N["gmax"], L.at("gmax", n + 1))
                    L.inc(act.activation(gexp[:], gexp[:], ACT.Exp), "act_misc")

                for t in range(4):
                    for c in range(4):
                        L.out(f"wq{4 * t + c}", qT[:, 4 * t + c, :], SEQ)
                    key_scores(t)
                L.hold(act, "act", "pj_full", GI[1]["s7"] + 1)
                for k in (6, 7, 4, 5):
                    key_scores(k)
                gate_exps(0)
                for tt in range(2):

                    def gelus(k0, last=False):
                        for g in range(GROUPS):
                            if g == GROUPS - 2 and not last:
                                gate_exps(k0 + 1)
                            act.wait_ge(N["u_free"], L.at("u_free", k0 * PART + GB * (g + 1)))
                            L.inc(act.activation(gl[:, g % 2, :], dots[:, g % 2, :], ACT.Gelu), "gelu_done")

                    per = {"u_free": PART, "gmax": 1, "act_misc": 1, "gelu_done": GROUPS}
                    L.turns(act, PAIRS - tt, per, lambda j: gelus(tt * PAIRS))
                    if tt:
                        gelus(2 * PAIRS - 1, last=True)
                    act.wait_ge(N["f_full"], L.at("f_full", tt + 1))
                    for n in range(2):
                        L.inc(act.activation(fn[:, n * 512:(n + 1) * 512], S[n][:], ACT.Copy), "f_read")
                    for hf in range(2):
                        L.out(f"ft{2 * tt + hf}", fT[tt][:, 4 * hf:4 * hf + 4, :], 512)
                L.pad()
                L.check(["evac", "sq_done", "e_done", "pt_read", "o_read", "act_misc", "gelu_done", "f_read"])

            def block2(l):
                L = Copies(2, l)
                def square_chunk(c, before):
                    act.wait_ge(N["x_done"], L.at("x_done", before + c + 1))
                    L.square(sq[:, c, :], xT[:, c, :])

                for c in range(KC):
                    square_chunk(c, -KC)
                L.mean("norm1", ms[:, 0, :], T2, D)
                for c in range(4):
                    L.out(f"cq{c}", cq[:, c, :], T2)
                L.evacuated(act, "cq3")
                L.square(sq[:, 0:4, :], cq)
                L.out("kpe", kpe[0:64, :], T2, m=64)
                for c in range(4):
                    L.out(f"rq{c}", rq[:, c, :], T2)
                L.mean("qa", ms[:, 0, :], T2, 256)
                L.mean("kva", ms[:, 1, :], T2, 256)
                L.out("kperm", tmpP[0:64, 4, :], T2, m=64)
                for c in range(4):
                    L.out(f"rk{c}", rk[:, c, :], T2)
                for t, (t0, m) in enumerate(ATILES):
                    L.out(f"rv{t}", rv[0:m, t, :], 512, m=m)
                for h in range(RH):
                    L.out(f"rqp{h}", tmpR[:, h, :], T2)
                for h in range(RH):
                    L.out(f"rkp{h}", tmpR[:, 4 + h, :], T2)
                for c in range(4):
                    b = L.src(f"rg{c}")
                    act.activation(rgt[:, c, :], b[:, 0:T2], ACT.Tanh, scale=0.5)
                    L.inc(act.activation(rgr[:, c, :], b[:, 0:T2], ACT.Copy, scale=0.5), "evac")
                for h in range(MH):
                    L.out(f"qn{h}", qn[:, h, :], T2)
                for h in range(MH):
                    L.out(f"qr{h}", qr[0:64, h, :], T2, m=64)
                for h in range(MH):
                    L.out(f"kn{h}", kn[:, h, :], T2)
                for t, (t0, m) in enumerate(ATILES):
                    L.out(f"v{t}", v2[0:m, t, :], 512, m=m)
                def outputs(u):
                    act.wait_ge(N["o_full"], L.at("o_full", u + 1))
                    L.inc(act.activation((ro if u < RH else mo)[:, u % 4, :], O[:, 0:T2], ACT.Copy), "o_read")

                L.evacuated(act, "kn3")
                for h, (dst, src) in enumerate(((sq[:, 0:4, :], qn), (sq[0:64, 4:8, :], qr[0:64, :, :]),
                                                (hT[:, 0:4, :], kn), (hT[0:64, 4, :], kpe[0:64, :]))):
                    L.square(dst, src)
                    outputs(h)
                for h in range(MH):
                    L.mean(f"qs{h}", ms[:, h, :], T2, QKH)
                for h in range(MH):
                    act.wait_ge(N["rstd"], L.at("rstd", 3 + h + 1))
                    L.mean(f"ks{h}", ms[:, h, :], T2, QKH)
                for h in range(MH):
                    L.out(f"qp{h}", tmpP[0:64, h, :], T2, m=64)

                for h in range(MH + 1):
                    if h < MH:
                        for r, (m, c0, n) in enumerate(((P, 0, P), (P, P, 2 * P), (16, 384, T2))):
                            if r == 0:
                                act.wait_ge(N["s_read"], L.at("s_read", RH + 2 * h + 1))
                                if h >= 2:
                                    act.wait_ge(N["p_done"], L.at("p_done", h - 1))
                            if r == 2:
                                act.wait_ge(N["s_read"], L.at("s_read", RH + 2 * h + 2))
                            L.inc(act.activation(ex[0:m, h % 2, c0:c0 + n], nl[0:m, h % 2, c0:c0 + n], ACT.Exp,
                                                 scale=-1.0, bias=nmax[0:m, h % 2, r:r + 1],
                                                 accum_out=esum[0:m, h % 2, r:r + 1]), "e_done")
                        L.out(f"rc{h}", ro[:, h, :], T2)
                        L.evacuated(act, f"rc{h}")
                        L.square(sq[:, h, :], ro[:, h, :])
                    else:
                        act.wait_ge(N["rstd"], L.at("rstd", 3 + 2 * MH))
                        for r in range(RH):
                            L.mean(f"rs{r}", ms[:, r, :], T2, P)
                    if h:
                        act.wait_ge(N["t_done"], L.at("t_done", h))
                        if h >= 3:
                            act.wait_ge(N["o_full"], L.at("o_full", RH + h - 2))
                        act.activation(pt[:, (h - 1) % 2, 0:416], PT[:, 0:416], ACT.Copy)
                        L.inc(act.activation(pt[0:16, (h - 1) % 2, 416:432], PT[0:16, 416:432], ACT.Copy), "pt_read")
                        outputs(RH + h - 1)
                        act.wait_ge(N["o_read"], L.at("o_read", RH + h))
                        L.square(sq[:, 4 + h - 1, :], mo[:, h - 1, :])
                for h in range(MH):
                    act.wait_ge(N["rstd"], L.at("rstd", 3 + 2 * MH + h + 1))
                    L.mean(f"ms{h}", ms[:, h, :], T2, P)
                for c in range(8):
                    L.out(f"out{c}", oTmp2[:, c, :], T2)
                    if c:
                        square_chunk(c - 1, 0)
                square_chunk(7, 0)
                L.mean("norm2", ms[:, 0, :], T2, D)
                for j in range(11):
                    if j >= 2:
                        act.wait_ge(N["b2_act"], L.at("b2_act", 2 * (j - 1)))
                    for i in range(2):
                        b = L.src(f"g{2 * j + i}")
                        act.activation(gbuf[:, j % 2, i, :], b[:, 0:T2], ACT.Tanh, scale=0.5)
                        L.inc(act.activation(gbuf[:, j % 2, 2 + i, :], b[:, 0:T2], ACT.Copy, scale=0.5), "evac")
                    for i in range(2):
                        L.out(f"u{2 * j + i}", gbuf[:, j % 2, 4 + i, :], T2)
                for c in range(8):
                    L.out(f"dn{c}", oTmp2[:, c, :], T2)
                L.pad()
                L.check(["evac", "sq_done", "e_done", "pt_read", "o_read", "act_misc", "gelu_done", "f_read"])

            with act.Fori(0, DEPTH) as l:
                block1(l)
            L = Copies("f", 0)
            L.square_all()
            L.mean("normf", ms[:, 0, 0:SEQ], SEQ, D)
            L.pad()
            with act.Fori(0, DEPTH) as l:
                block2(l)

        @block.vector
        def _(dve):
            tt_ = dve.tensor_tensor
            stt = dve.scalar_tensor_tensor
            dve.memset(ones[:], 1.0)
            dve.memset(loff[:], 0.0)
            dve.memset(eps[:, 2:3], 0.0)
            dve.memset(eps[:, 0:1], EPS)
            dve.memset(eps[:, 1:2], 1.0).then_inc(memset_done, 1)
            dve.wait_ge(const_full, 96)
            dve.wait_ge(memset_done, 1)
            dve.tensor_scalar(nsel[:], kst[0:FH, K_ID:K_ID + FH], -1.0, None, ALU.mult)
            dve.sem_inc(N["x_done"], 2)
            dve.wait_ge(setup_pe, 2)
            for h in range(DH):
                f = S[h // 2][:, 256 * (h % 2):256 * (h % 2) + 256]
                tt_(bias[:, h, 0:P], f[:, P:2 * P], mask[:, 0:P], ALU.add)
                tt_(bias[:, h, P:2 * P], f[:, 0:P], mask[:, P:2 * P], ALU.add)
                m = tt_(bias[:, h, 2 * P:3 * P], f[:, P:2 * P], mask[:, 2 * P:3 * P], ALU.add)
            m.then_inc(setup_dve, 1)
            dve.wait_ge(setup_dve, 1)
            dve.sem_inc(N["s_read"], 2)
            dve.sem_inc(N["u_free"], UB)
            dve.sem_inc(N["diag_done"], 1)

            class Steps(Layer):
                def step(self, ins):
                    self.inc(ins, "dve_misc")

                def settle(self, held_=False):
                    k = self.n["dve_misc"]
                    (self.hold(dve, "dve", "dve_misc", k) if held_ else dve.wait_ge(N["dve_misc"], self.at("dve_misc", k)))

                def root(self, group, i, o, n):
                    self.evacuated(dve, group)
                    if not group.startswith("norm"):
                        self.inc(dve.reciprocal(rstd[:, o, 0:n], ms[:, i, 0:n]), "rstd")
                        dve.wait_ge(N["rstd"], self.at("rstd", self.n["rstd"]))
                        return
                    r, t, m = rstd[:, o, 0:n], ms[:, i, 0:n], rstd[:, 7, 0:n]
                    self.step(dve.reciprocal(r, t))
                    self.settle()
                    self.step(stt(t, m, -0.5, r, ALU.mult, ALU.mult))
                    self.settle()
                    self.step(tt_(t, t, r, ALU.mult))
                    self.settle()
                    self.inc(stt(r, t, 1.5, r, ALU.add, ALU.mult), "rstd")
                    dve.wait_ge(N["rstd"], self.at("rstd", self.n["rstd"]))

                def norm(self, dst, src, gain, r, name):
                    for c in range(len(dst)):
                        self.inc(stt(dst[c], src[c], gain[c], r, ALU.mult, ALU.mult), name)

            def block1(l):
                L = Steps(1, l)
                dve.wait_ge(N["cols_full"], L.at("cols_full", 16))
                for a in range(2):
                    o = C1_LAM + 128 * a
                    m = dve.tensor_tensor_reduce(out=junk[:, 64 * a:64 * a + 64], in0=cols[:, o:o + 64],
                                                 in1=cols[:, o + 64:o + 128],
                                                 scale=1.0, scalar=0.0, op0=ALU.mult, op1=ALU.add,
                                                 accum_out=lam[:, a:a + 1])
                L.inc(m, "l_done")
                L.root("norm1", 0, 0, SEQ)
                L.norm([hT[:, c, TX] for c in range(KC)], [xT[:, c, TX] for c in range(KC)],
                       [cols[:, C1_N1 + c:C1_N1 + c + 1] for c in range(KC)], rstd[:, 0, 0:SEQ], "h_done")
                L.evacuated(dve, "ff")
                L.step(dve.tensor_scalar(fox[:, 1, :], fox[:, 0, :], 0.0, None, ALU.min))
                L.settle()
                L.inc(stt(fox[:, 2, :], fox[:, 1, :], -2.0, fox[:, 0, :], ALU.mult, ALU.add), "z_done")
                dve.wait_ge(N["act_misc"], L.at("act_misc", 1))
                L.step(tt_(lam[:, 4:5], lam[:, 3:4], lam[:, 2:3], ALU.subtract))
                L.settle()
                tt_(lam[:, 5:6], lam[:, 4:5], cols[:, C1_LI:C1_LI + 1], ALU.subtract)
                L.step(tt_(lam[:, 6:7], cols[:, C1_SUB:C1_SUB + 1], cols[:, C1_LI + 1:C1_LI + 2], ALU.mult))
                dve.wait_ge(N["act_misc"], L.at("act_misc", 3))
                L.step(tt_(fox[:, 4, :], fox[:, 1, :], fox[:, 4, :], ALU.subtract))
                L.settle()
                L.inc(dve.tensor_tensor_scan(fox[:, 5, :], eps[0:FH, 1:2].to_broadcast([FH, SEQ]), fox[:, 4, :], 0.0,
                                             ALU.mult, ALU.add), "c_done")

                def logits(i):
                    dve.wait_ge(N["s_full"], L.at("s_full", i + 1))
                    dve.sem_inc(held["dve"], 1)
                    if i >= 2:
                        L.hold(dve, "dve", "e_done", 2 * (i - 1))
                    b = bias[:, i // 2, :] if i < 2 * DH else mask
                    for r, (c0, n) in enumerate(((0, P), (P, 2 * P))):
                        m = dve.tensor_tensor_reduce(out=nl[:, i % 2, c0:c0 + n], in0=S[i % 2][:, c0:c0 + n],
                                                     in1=b[:, c0:c0 + n], scale=-1.0, scalar=BIG, op0=ALU.add,
                                                     op1=ALU.min, accum_out=nmax[:, i % 2, r:r + 1])
                    L.inc(m, "s_read")

                def probs(i):
                    p, u = i % 2, UNIT.get(i, i // 2)
                    dve.wait_ge(N["e_done"], L.at("e_done", 2 * (i + 1)))
                    L.step(dve.reciprocal(erec[:, p, 0:2], esum[:, p, 0:2]))
                    L.settle()
                    if i < 2 * DH and i % 2:
                        L.step(dve.tensor_scalar(erec[:, p, 0:2], erec[:, p, 0:2], lam[:, 5:6], None, ALU.mult))
                        L.settle()
                        for r, (c0, n) in enumerate(((0, P), (P, 2 * P))):
                            m = stt(pr[:, u % 2, c0:c0 + n], ex[:, p, c0:c0 + n], erec[:, p, r:r + 1],
                                    pr[:, u % 2, c0:c0 + n], ALU.mult, ALU.add)
                    else:
                        if u >= 2:
                            dve.wait_ge(N["t_done"], L.at("t_done", u - 1))
                        for r, (c0, n) in enumerate(((0, P), (P, 2 * P))):
                            m = dve.tensor_scalar(pr[:, u % 2, c0:c0 + n], ex[:, p, c0:c0 + n], erec[:, p, r:r + 1],
                                                  None, ALU.mult)
                    L.inc(m, "p_done")

                for i in range(MAPS + 1):
                    if i < MAPS:
                        logits(i)
                    if i:
                        probs(i - 1)

                dve.wait_ge(N["h_done"], L.at("h_done", KC))
                for h in range(DH):
                    L.root(f"dnorm{h}", h, h, SEQ)
                    L.inc(stt(ydT[:, h, :], ydT[:, h, :], lam[:, 6:7], rstd[:, h, 0:SEQ], ALU.mult, ALU.mult), "y_done")
                for c in range(8):
                    L.evacuated(dve, f"do{c}")
                    stt(doT[:, c, :], gate[:, c, :], 1.0, doT[:, c, :], ALU.add, ALU.mult)
                    L.step(stt(foT[:, c, :], gate[:, 8 + c, :], 1.0, foT[:, c, :], ALU.add, ALU.mult))
                    L.settle()
                    L.inc(tt_(mgT[:, c, :], doT[:, c, :], foT[:, c, :], ALU.add), "y_done")
                for c in range(8):
                    L.evacuated(dve, f"out{c}")
                    L.inc(tt_(xT[:, c, TX], xT[:, c, TX], oTmp[:, c, :], ALU.add), "x_done")
                dve.wait_ge(N["y_done"], L.at("y_done", DH))
                L.root("norm2", 0, 0, SEQ)
                L.norm([hT[:, c, TX] for c in range(KC)], [xT[:, c, TX] for c in range(KC)],
                       [cols[:, C1_N2 + c:C1_N2 + c + 1] for c in range(KC)], rstd[:, 0, 0:SEQ], "h_done")

                def top16(src, vals, poss):
                    for a in range(2):
                        for v, x in zip(vals, src):
                            m = dve.max(v[:, 8 * a:8 * a + 8], x)
                        L.step(m)
                        L.settle(True)
                        for v, x, q in zip(vals, src, poss):
                            m = dve.max_index(q[:, 8 * a:8 * a + 8], v[:, 8 * a:8 * a + 8], x)
                        L.step(m)
                        if a == 0:
                            L.settle(True)
                            for v, x in zip(vals, src):
                                m = dve.match_replace(x, v[:, 0:8], x, -3e38)
                            L.step(m)
                            L.settle(True)

                rows = lambda x, n: [x[:, i, :] for i in range(n)]

                def best_keys(at):
                    L.settle()
                    L.step(dve.tensor_scalar(work[:, :, :].rearrange("p a n -> p (a n)"), at, 1.0, None, ALU.mult))
                    L.settle(True)
                    top16(rows(work, 4), rows(topv, 4), rows(topi, 4))
                    L.settle()

                def best_pairs():
                    t4 = lambda x: x.rearrange("p (h a) k -> p h a k", a=2)
                    dve.tensor_scalar(t4(topf)[:, :, 0, :], t4(topi)[:, :, 0, :], 128.0, loff[:, 0:1], ALU.mult, ALU.add)
                    L.step(dve.tensor_copy(t4(topf)[:, :, 1, :], t4(topi)[:, :, 1, :]))
                    L.settle()
                    for dst, src in ((cnd, topv), (cidx, topf)):
                        off = 0
                        for i0, ni, nj in RANKS:
                            m = tt_(dst[:, :, off:off + ni * nj].rearrange("p h (a b) -> p h a b", a=ni),
                                    t4(src)[:, :, 0, i0:i0 + ni].unsqueeze(3).to_broadcast([P, 2, ni, nj]),
                                    t4(src)[:, :, 1, 0:nj].unsqueeze(2).to_broadcast([P, 2, ni, nj]), ALU.add)
                            off += ni * nj
                    L.step(m)
                    L.settle(True)
                    top16(rows(cnd, 2), rows(bestv, 2), rows(bestp, 2))
                    L.settle()

                def best_experts(k0):
                    L.step(dve.tensor_copy(bestf, bestp))
                    L.inc(tt_(gexp, bestv, bestv[:, :, 0:1].to_broadcast([P, 2, TOPK]), ALU.subtract), "gmax")
                    L.settle()
                    L.step(tt_(eq, iota.unsqueeze(1).to_broadcast([P, PART, CAND]),
                               bestf.rearrange("p h k -> p (h k)").unsqueeze(2).to_broadcast([P, PART, CAND]), ALU.is_equal))
                    L.settle()
                    e4 = eq.rearrange("p (h k) c -> p h k c", h=2)
                    L.step(tt_(e4, e4, cidx.unsqueeze(2).to_broadcast([P, 2, TOPK, CAND]), ALU.mult))
                    L.settle()
                    if k0 is not None:
                        dve.wait_ge(N["idx_b"], L.at("idx_b", k0 + 1))
                    L.step(dve.tensor_reduce(idxf[:], eq, AX.X, ALU.add))
                    L.settle()

                def next_gates(n):
                    dve.wait_ge(N["act_misc"], L.at("act_misc", 3 + n + 1))
                    L.step(dve.tensor_reduce(gsum[:, 0, :], gexp, AX.X, ALU.add))
                    L.settle()
                    L.step(dve.reciprocal(gsum[:, 1, :], gsum[:, 0, :]))
                    L.settle()
                    L.step(tt_(gnext, gexp, gsum[:, 1, :].unsqueeze(2).to_broadcast([P, 2, TOPK]), ALU.mult))
                    L.settle()

                def take_gates():
                    L.step(dve.tensor_copy(gates, gnext.rearrange("p h k -> p (h k)")))

                def turn(k0, j, last=False):
                    tt = k0 // PAIRS
                    for g in range(GROUPS):
                        for i in range(GB):
                            b = GB * (g % 2) + i
                            dve.wait_ge(u_full[b], L.l * (32 * SLOTS // UB) + j * (16 * PART // UB)
                                        + 16 * (k0 * PART // UB + g // 2 + 1))
                            L.inc(dve.tensor_tensor_reduce(out=urow[:, b, :], in0=urow[:, b, :], in1=h2n[:, tt, :],
                                                           scale=1.0, scalar=0.0, op0=ALU.mult, op1=ALU.add,
                                                           accum_out=dots[:, g % 2, i:i + 1]), "u_free")
                        if g == 1:
                            dve.wait_ge(N["v_free"], L.at("v_free", k0 * PART))
                            L.inc(dve.tensor_scalar(idx[:, TOPK:PART], idxf[:, TOPK:PART], 0.0, None, ALU.add), "idx_b")
                        if g == 5 and not last:
                            dve.wait_ge(N["v_free"], L.at("v_free", k0 * PART + 4 * GB))
                            L.inc(dve.tensor_scalar(idx[:, 0:TOPK], idxf[:, 0:TOPK], 0.0, None, ALU.add), "idx_a")
                        dve.wait_ge(N["gelu_done"], L.at("gelu_done", k0 * GROUPS + g + 1))
                        dve.wait_ge(N["diag_done"], L.at("diag_done", k0 * PART + GB * g))
                        if g == 0:
                            L.settle()
                        L.step(tt_(wgt[:, g % 2, :], gl[:, g % 2, :], gates[:, GB * g:GB * g + GB], ALU.mult))
                        L.settle()
                        dve.wait_ge(N["v_free"], L.at("v_free", k0 * PART + GB * (g - 1)))
                        for i in range(GB):
                            b = GB * (g % 2) + i
                            L.inc(dve.tensor_scalar(diag[:, b, :], ident, wgt[:, g % 2, i:i + 1], None, ALU.mult), "diag_done")
                        if last:
                            continue
                        if g == 2:
                            o = keys_at(k0 + 1)
                            at = area2[:, o:o + 512] if isinstance(j, int) else area2[:, bass.ds(j * -512 + o, 512)]
                            best_keys(at)
                        if g == 3:
                            best_pairs()
                        if g == 4:
                            best_experts(k0)
                        if g == GROUPS - 1:
                            next_gates(k0 + 1)
                            take_gates()

                L.evacuated(dve, "s0")
                best_keys(area2[:, keys_at(0):keys_at(0) + 512])
                best_pairs()
                best_experts(None)
                L.inc(dve.tensor_copy(idx[:, 0:TOPK], idxf[:, 0:TOPK]), "idx_a")
                L.hold(dve, "dve", "evac", GI[1]["s5"] + 1)
                next_gates(0)
                take_gates()
                per = {"dve_misc": TURN_STEPS, "u_free": PART, "diag_done": PART, "idx_a": 1, "idx_b": 1, "gmax": 1,
                       "v_free": PART, "gelu_done": GROUPS, "act_misc": 1}
                L.turns(dve, PAIRS, per, lambda j: turn(0, j))
                L.turns(dve, PAIRS - 1, per, lambda j: turn(PAIRS, j))
                turn(2 * PAIRS - 1, 0, last=True)
                for tt in range(2):
                    for hf in range(2):
                        L.evacuated(dve, f"ft{2 * tt + hf}")
                        x = xT[:, 4 * hf:4 * hf + 4, META + tt * P:META + (tt + 1) * P]
                        L.inc(tt_(x, x, fT[tt][:, 4 * hf:4 * hf + 4, :], ALU.add), "x_done")
                L.step(dve.tensor_scalar(loff[:], loff[:], float(NEXP), None, ALU.add))
                L.check(["rstd", "h_done", "s_read", "p_done", "x_done", "y_done", "c_done", "z_done", "l_done", "gmax", "idx_a",
                         "idx_b", "u_free", "diag_done", "dve_misc"])

            def block2(l):
                L = Steps(2, l)
                col = lambda c, m=P: cols[0:m, c:c + 1]
                dve.wait_ge(N["cols_full"], L.at("cols_full", 16))
                L.inc(dve.tensor_scalar(lam[:, 0:2], cols[:, C2_QG:C2_QG + 2], QKH ** -0.5, None, ALU.mult), "small_done")
                L.root("norm1", 0, 0, T2)
                L.norm([hT[:, c, :] for c in range(KC)], [xT[:, c, :] for c in range(KC)],
                       [col(C2_N1 + c) for c in range(KC)], rstd[:, 0, :], "h_done")
                L.evacuated(dve, "kpe")
                L.inc(dve.tensor_scalar(kpg[0:64, :], kpe[0:64, :], col(C2_KG + 1, 64), None, ALU.mult), "small_done")
                dve.wait_ge(const2_full, 16)
                dve.wait_ge(N["small_done"], L.at("small_done", 2))
                L.inc(tt_(kro[0:64, :], kpg[0:64, :], cosM, ALU.mult), "small_done")
                L.root("qa", 0, 1, T2)
                L.root("kva", 1, 2, T2)
                L.norm([cq[:, c, :] for c in (0, 1)], [cq[:, c, :] for c in (0, 1)], [col(C2_QA + c) for c in range(2)],
                       rstd[:, 1, :], "small_done")
                L.norm([cq[:, c, :] for c in (2, 3)], [cq[:, c, :] for c in (2, 3)], [col(C2_KVA + c) for c in range(2)],
                       rstd[:, 2, :], "small_done")
                L.evacuated(dve, "kperm")
                L.step(tt_(tmpP[0:64, 4, :], tmpP[0:64, 4, :], sinM, ALU.mult))
                L.settle()
                L.step(tt_(kro[0:64, :], kro[0:64, :], tmpP[0:64, 4, :], ALU.add))

                def rotate(x, t, c, s):
                    tt_(t, t, s, ALU.mult)
                    L.step(tt_(x, x, c, ALU.mult))
                    L.settle()
                    return tt_(x, x, t, ALU.add)

                for h in range(RH):
                    L.evacuated(dve, f"rkp{h}")
                    for x, t in ((rq, h), (rk, 4 + h)):
                        L.inc(rotate(x[:, h, :], tmpR[:, t, :], cosR, sinR), "rot_done")
                L.evacuated(dve, "rg3")
                for h in range(RH):
                    L.step(stt(rgr[:, h, :], rgt[:, h, :], 1.0, rgr[:, h, :], ALU.add, ALU.mult))
                for h in range(RH):
                    dve.wait_ge(N["s_full"], L.at("s_full", h + 1))
                    if h >= 2:
                        dve.wait_ge(N["o_full"], L.at("o_full", h - 1))
                    dh = k2st[:, K2_D + 432 * h:K2_D + 432 * (h + 1)]
                    tt_(pr[:, h % 2, 0:416], S[h % 2][:, 0:416], dh[:, 0:416], ALU.mult)
                    L.inc(tt_(pr[0:16, h % 2, 416:432], S[h % 2][0:16, 416:432], dh[0:16, 416:432], ALU.mult), "s_read")
                dve.wait_ge(N["small_done"], L.at("small_done", 7))
                for h in range(MH):
                    L.root(f"qs{h}", h, h, T2)
                    L.step(stt(qn[:, h, :], qn[:, h, :], lam[:, 0:1], rstd[:, h, :], ALU.mult, ALU.mult))
                    L.inc(stt(qr[0:64, h, :], qr[0:64, h, :], lam[0:64, 1:2], rstd[0:64, h, :], ALU.mult, ALU.mult), "small_done")
                for h in range(MH):
                    L.root(f"ks{h}", h, 4 + h, T2)
                    L.step(stt(kn[:, h, :], kn[:, h, :], col(C2_KG), rstd[:, 4 + h, :], ALU.mult, ALU.mult))
                    L.inc(tt_(kr[0:64, h, :], kro[0:64, :], rstd[0:64, 4 + h, :], ALU.mult), "rot_done")
                    L.evacuated(dve, f"qp{h}")
                    L.inc(rotate(qr[0:64, h, :], tmpP[0:64, h, :], cosM, sinM), "rot_done")

                REG = ((P, 0, P, 0), (P, P, 2 * P, 0), (16, 384, T2, 1))

                def logits(h):
                    use = RH + 2 * h
                    if h == 0:
                        dve.wait_ge(N["o_full"], L.at("o_full", RH))
                    if h >= 2:
                        L.hold(dve, "dve", "e_done", 3 * (h - 1))
                    for r, (m, c0, n, bk) in enumerate(REG):
                        if r != 1:
                            L.hold(dve, "dve", "s_full", use + bk + 1)
                        s0 = 0 if r == 2 else c0
                        i = dve.tensor_tensor_reduce(out=nl[0:m, h % 2, c0:c0 + n], in0=S[(use + bk) % 2][0:m, s0:s0 + n],
                                                     in1=k2st[0:m, K2_MASK:K2_MASK + n] if r == 2 else mask[:, c0:c0 + n], scale=-1.0, scalar=BIG,
                                                     op0=ALU.add, op1=ALU.min, accum_out=nmax[0:m, h % 2, r:r + 1])
                        if r:
                            L.inc(i, "s_read")

                def probs(h):
                    p = h % 2
                    dve.wait_ge(N["e_done"], L.at("e_done", 3 * (h + 1)))
                    dve.reciprocal(erec[:, p, 0:2], esum[:, p, 0:2])
                    L.step(dve.reciprocal(erec[0:16, p, 2:3], esum[0:16, p, 2:3]))
                    if h >= 2:
                        dve.wait_ge(N["t_done"], L.at("t_done", h - 1))
                    L.settle()
                    for r, (m, c0, n, bk) in enumerate(REG):
                        i = dve.tensor_scalar(pr[0:m, p, c0:c0 + n], ex[0:m, p, c0:c0 + n], erec[0:m, p, r:r + 1], None,
                                              ALU.mult)
                    L.inc(i, "p_done")

                for h in range(MH + 1):
                    if h < MH:
                        logits(h)
                    if h:
                        probs(h - 1)
                for h in range(RH):
                    L.root(f"rs{h}", h, h, T2)
                    L.step(stt(ro[:, h, :], ro[:, h, :], col(C2_RG + h), rstd[:, h, :], ALU.mult, ALU.mult))
                    L.settle()
                    L.inc(stt(yT[:, 4 + h, :], ro[:, h, :], col(C2_RB + h), rgr[:, h, :], ALU.add, ALU.mult), "y_done")
                for h in range(MH):
                    L.root(f"ms{h}", h, 4 + h, T2)
                    L.inc(stt(yT[:, h, :], mo[:, h, :], col(C2_MO + h), rstd[:, 4 + h, :], ALU.mult, ALU.mult), "y_done")
                for c in range(8):
                    L.evacuated(dve, f"out{c}")
                    L.inc(tt_(xT[:, c, :], xT[:, c, :], oTmp2[:, c, :], ALU.add), "x_done")
                L.root("norm2", 0, 0, T2)
                L.norm([hT[:, c, :] for c in range(KC)], [xT[:, c, :] for c in range(KC)],
                       [col(C2_N2 + c) for c in range(KC)], rstd[:, 0, :], "h_done")
                for j in range(11):
                    for i in range(2):
                        g = gbuf[:, j % 2, :, :]
                        L.evacuated(dve, f"u{2 * j + i}")
                        L.step(stt(g[:, i, :], g[:, i, :], 1.0, g[:, 2 + i, :], ALU.add, ALU.mult))
                        L.settle()
                        L.inc(tt_(actT[:, 2 * j + i, :], g[:, i, :], g[:, 4 + i, :], ALU.mult), "b2_act")
                for c in range(8):
                    L.evacuated(dve, f"dn{c}")
                    L.inc(tt_(xT[:, c, :], xT[:, c, :], oTmp2[:, c, :], ALU.add), "x_done")
                L.check(["rstd", "h_done", "s_read", "p_done", "x_done", "y_done", "small_done", "rot_done", "b2_act", "dve_misc"])

            with dve.Fori(0, DEPTH) as l:
                block1(l)
            L = Steps("f", 0)
            L.root("normf", 0, 0, SEQ)
            L.norm([xT[:, c, TX] for c in range(KC)], [xT[:, c, TX] for c in range(KC)],
                   [fing[:, c:c + 1] for c in range(KC)], rstd[:, 0, 0:SEQ], "x_done")
            with dve.Fori(0, DEPTH) as l:
                block2(l)

        @block.gpsimd
        def _(pool):
            pool.wait_ge(memset_done, 1)
            table_u, table_v = (t.rearrange("l e d -> (l e) d") for t in (eu, ev))

            def params(L, src, n):
                L.hold(pool, "pool", "x_done", 0)
                L.inc(pool.dma_start(cols[:, 0:n], src[L.l, :, :]), "cols_full", 16)

            def gather(rows, table, col, b, full):
                pool.indirect_dma_start(out=rows[:, b, :], out_offset=None, in_=table,
                                        in_offset=bass.IndirectOffsetOnAxis(ap=idx[:, col:col + 1], axis=0))\
                    .then_inc(full[b], 16)

            def block1(l):
                L = Layer(1, l)
                params(L, c1_in, NC1)
                for tt in range(2):
                    with pool.Fori(0, SLOTS // (8 * GB)) as j:
                        def rows_u(g):
                            if g == 0:
                                pool.wait_ge(N["idx_a"], L.at("idx_a", tt * PAIRS + 1) + j)
                            if g == 4:
                                pool.wait_ge(N["idx_b"], L.at("idx_b", tt * PAIRS + 1) + j)
                                pool.sem_inc(held["pool"], 1)
                            pool.wait_ge(N["u_free"], L.at("u_free", tt * SLOTS + GB * (g - 1)) + j * (8 * GB))
                            pool.sem_inc(held["pool"], 1)
                            for i in range(GB):
                                gather(urow, table_u, GB * g + i, GB * (g % 2) + i, u_full)

                        def rows_v(g):
                            pool.wait_ge(N["v_free"], L.at("v_free", tt * SLOTS + GB * (g - 1)) + j * (8 * GB))
                            pool.sem_inc(held["pool"], 1)
                            for i in range(GB):
                                gather(vrow, table_v, GB * g + i, GB * (g % 2) + i, v_full)

                        rows_u(0)
                        for g in range(8):
                            if g < 7:
                                rows_u(g + 1)
                            rows_v(g)
                L.check(["cols_full"])

            def block2(l):
                L = Layer(2, l)
                params(L, c2_in, NC2)
                L.check(["cols_full"])

            with pool.Fori(0, DEPTH) as l:
                block1(l)
            L = Layer("f", 0)
            pool.wait_ge(N["x_done"], L.at("x_done", 0))
            pool.dma_start(k2st, k2_in).then_inc(const2_full, 16)
            with pool.Fori(0, DEPTH) as l:
                block2(l)


def chunks(w, n):
    k = w.shape[0] // P
    return w.reshape(k, P, w.shape[1] // n, n).transpose(2, 1, 0, 3).reshape(w.shape[1] // n, P, k * n)


def wide(t):
    out = np.zeros(t.shape[:-1] + (TILE,), t.dtype)
    out[..., :t.shape[-1]] = t
    return out


def column(v, rows=P):
    return v.reshape(-1, rows).T


def layout_stream(a):
    tiles = []
    for l in range(DEPTH):
        w = a["w_in"][l]
        cut = np.cumsum([512, 512, 512, 512, 512, 512, FH])
        dq, dk, dv_, fq, fk, fv_, ff, gates_ = np.split(w, cut, axis=1)
        for x in (dq, dk, dv_, fq, fk, fv_, gates_):
            tiles.append(chunks(x, 512))
        tiles.append(chunks(a["w_fox_o"][l], 1024))
        tiles.append(chunks(a["w_diff_o"][l], 1024))
        tiles.append(chunks(a["w_out"][l], 512))
        tiles.append(chunks(a["w_query"][l], 512))
    for l in range(DEPTH):
        w = a["w_in_2"][l]
        tiles.append(chunks(w[:, 0:512], 512))
        tiles.append(chunks(w[:, 576:2624], 512))
        q = a["w_q_b_2"][l].reshape(256, MH, QKH)
        q = np.concatenate([q[:, :, :P].reshape(256, -1), q[:, :, P:].reshape(256, -1)], axis=1)
        kv = a["w_kv_b_2"][l].reshape(256, MH, 2 * P)
        kv = np.concatenate([kv[:, :, :P].reshape(256, -1), kv[:, :, P:].reshape(256, -1)], axis=1)
        tiles.append(wide(np.concatenate([chunks(q, 768), chunks(kv, 1024)], axis=2)))
        tiles.append(chunks(a["w_out_2"][l], 512))
        gu = a["w_gate_up_2"][l].reshape(D, 2, DFF // 256, 256).transpose(0, 2, 1, 3).reshape(D, 2 * DFF)
        tiles.append(chunks(gu, 512))
        tiles.append(wide(chunks(a["w_down_2"][l], P)))
    return np.concatenate(tiles, axis=0)


def layout_cols1(a):
    out = np.zeros((DEPTH, P, NC1), np.float32)
    for l in range(DEPTH):
        o = out[l]
        o[:, C1_N1:C1_N1 + 8] = column(a["norm1_g"][l])
        o[:, C1_N2:C1_N2 + 8] = column(a["norm2_g"][l])
        o[:, C1_SUB] = a["diff_subln_g"][l]
        o[:, C1_LAM:C1_LAM + 256] = a["diff_lambda"][l].reshape(1, 256)
        o[:FH, C1_BF] = a["b_forget"][l]
        li = 0.8 - 0.6 * math.exp(-0.3 * l)
        o[:, C1_LI] = li
        o[:, C1_LI + 1] = 1.0 - li
        o[:, C1_FF:C1_FF + 64] = a["w_in"][l][:, 3072:3080].reshape(KC, P, FH).transpose(1, 0, 2).reshape(P, 64)
        o[:, C1_KEY:C1_KEY + 256] = a["sub_keys"][l].transpose(2, 0, 1).reshape(P, 256)
    return out


def layout_cols2(a):
    out = np.zeros((DEPTH, P, NC2), np.float32)
    for l in range(DEPTH):
        o = out[l]
        for at, name in ((C2_N1, "attn_norm_g_2"), (C2_N2, "ffn_norm_g_2"), (C2_QA, "q_a_norm_g_2"),
                         (C2_KVA, "kv_a_norm_g_2"), (C2_MO, "mla_out_norm_g_2"), (C2_RG, "ret_norm_g_2"),
                         (C2_RB, "ret_norm_b_2")):
            c = column(a[name][l])
            o[:, at:at + c.shape[1]] = c
        for at, name in ((C2_QG, "q_norm_g_2"), (C2_KG, "k_norm_g_2")):
            o[:, at] = a[name][l][:P]
            o[:64, at + 1] = a[name][l][P:]
        o[:, C2_KPE:] = a["w_in_2"][l][:, 512:576].reshape(KC, P, 64).transpose(1, 0, 2).reshape(P, KC * 64)
    return out


def constants1():
    k = np.zeros((P, NK1), np.float32)
    p = np.arange(P)
    k[:, K_ID:K_ID + P] = np.eye(P)
    k[:, K_FLIP:K_FLIP + P] = np.eye(P)[::-1]
    k[:, K_CEN:K_CEN + P] = np.eye(P) - 1.0 / P
    k[:, K_PM:K_PM + P] = np.roll(np.eye(P), 64, axis=1)
    k[:64, K_PR:K_PR + 64] = np.roll(np.eye(64), 32, axis=1)
    causal = np.where(p[:, None] >= p[None, :], 0.0, NEG)
    k[:, K_MASK:K_MASK + P] = causal
    k[:, K_MASK + 2 * P:K_MASK + 3 * P] = causal
    k[:, K_IOTA:K_IOTA + CAND] = np.arange(CAND)
    y = np.arange(384)
    dist = np.maximum(255 - y, 0)
    exact = BUCKETS // 2
    nf = np.maximum(dist, 1).astype(np.float32)
    large = exact + (np.log(nf / exact) / np.float32(math.log(MAX_DIST / exact)) * (BUCKETS - exact)).astype(np.int32)
    bucket = np.where(dist < exact, dist, np.minimum(large, BUCKETS - 1))
    k[:BUCKETS, K_OH:K_OH + 384] = bucket[None, :] == np.arange(BUCKETS)[:, None]
    return k


def constants2():
    k = np.zeros((P, NK2), np.float32)
    p = np.arange(P)
    for h in range(RH):
        lg = math.log(1.0 - 2.0 ** (-5.0 - h))
        for t, (m, n0, c0) in enumerate(((P, 0, 0), (P, P, T2), (16, 2 * P, 416))):
            diff = np.arange(n0, T2)[None, :] - (t * P + p[:m])[:, None]
            d = np.where(diff >= 0, np.exp(np.maximum(diff, 0) * lg), 0.0) * P ** -0.5
            k[:m, K2_D + 432 * h + c0:K2_D + 432 * h + c0 + T2 - n0] = d
    pos = np.arange(T2, dtype=np.float32)
    for dim, c, s in ((128, K2_CR, K2_SR), (64, K2_CM, K2_SM)):
        inv = (np.float32(10000.0) ** (-np.arange(0, dim, 2, dtype=np.float32) / dim)).astype(np.float32)
        ang = (pos[None, :] * inv[:, None]).astype(np.float32)
        k[:dim, c:c + T2] = np.concatenate([np.cos(ang), np.cos(ang)])
        k[:dim, s:s + T2] = np.concatenate([-np.sin(ang), np.sin(ang)])
    k[:16, K2_MASK:K2_MASK + T2] = np.where((2 * P + p[:16])[:, None] >= np.arange(T2)[None, :], 0.0, NEG)
    return k


def kernel(**inputs):
    import concourse.bacc as bacc
    from concourse.bass_utils import run_bass_kernel_spmd

    a = {k: np.asarray(v) for k, v in inputs.items()}
    feed = {
        "x": a["x"][0].T.reshape(KC, P, SEQ).transpose(1, 0, 2),
        "meta": a["meta_tokens_2"].T.reshape(KC, P, META).transpose(1, 0, 2),
        "weights": layout_stream(a),
        "cols1": layout_cols1(a),
        "cols2": layout_cols2(a),
        "final_g": column(a["final_norm_g"]),
        "rel_bias": a["rel_bias"],
        "const1": constants1(),
        "const2": constants2(),
        "expert_u": a["expert_u"],
        "expert_v": a["expert_v"],
    }
    nc = bacc.Bacc("TRN2", target_bir_lowering=False, num_devices=1)
    arrays, args = {}, []
    for name, v in feed.items():
        v = np.ascontiguousarray(v)
        arrays[f"in_{name}"] = v
        args.append(nc.dram_tensor(f"in_{name}", v.shape, mybir.dt.from_np(v.dtype), kind="ExternalInput").ap())
    args.append(nc.dram_tensor("out_x", (P, KC, SEQ), F32, kind="ExternalOutput").ap())
    program(nc, *args)
    r = run_bass_kernel_spmd(nc, [arrays], core_ids=[0])
    got = np.asarray(r.results[0]["out_x"])
    return np.ascontiguousarray(got.transpose(2, 1, 0).reshape(1, SEQ, D))
```
